# Optimizing a Trainium2 kernel written in Bass

```python
import math
import jax
import jax.numpy as jnp
from jax import lax
import numpy as np

D_MODEL = 2048
BATCH = 1
SEQ = 512
DEPTH = 1
DEC_BATCH = 1
DEC_SEQ = 32
PAST_LEN = 512

CHUNK = 64
RMS_EPS = 1e-6
GDN_HEADS = 8
GDN_HEAD_DIM = 128
GDN_WIDTH = GDN_HEADS * GDN_HEAD_DIM
GDN_CONV = 4
GDN_CONV_DIM = 3 * GDN_WIDTH
DIFF_HEADS = 8
DIFF_HEAD_DIM = 64
DIFF_V_DIM = 2 * DIFF_HEAD_DIM
DIFF_QK_WIDTH = DIFF_HEADS * 2 * DIFF_HEAD_DIM
DIFF_WIDTH = DIFF_HEADS * DIFF_V_DIM
ATTN_BLOCK = 128
MEM_TOKENS = 256
MEM_HEADS = 4
MEM_HEAD_DIM = D_MODEL // MEM_HEADS
PEER_HEADS = 8
PEER_N_KEYS = 128
PEER_EXPERTS = PEER_N_KEYS * PEER_N_KEYS
PEER_TOPK = 16
PEER_QUERY_DIM = 256
PEER_HALF = PEER_QUERY_DIM // 2
PEER_BLOCK = 128
IN_SIZES = (GDN_CONV_DIM, GDN_WIDTH, GDN_HEADS, GDN_HEADS, DIFF_QK_WIDTH, DIFF_QK_WIDTH, DIFF_WIDTH, D_MODEL, D_MODEL)
IN_COLS = sum(IN_SIZES)

kernel_name = 'hybrid_stream_gdn_diffattn_peer_step'

def rmsnorm(x, g):
    xf = x.astype(jnp.float32)
    y = xf * lax.rsqrt(jnp.mean(xf * xf, axis=-1, keepdims=True) + RMS_EPS)
    return (y * g.astype(jnp.float32)).astype(x.dtype)

def l2norm(x):
    xf = x.astype(jnp.float32)
    return xf * lax.rsqrt(jnp.sum(xf * xf, axis=-1, keepdims=True) + 1e-6)

def alibi_slopes(n):
    return jnp.asarray(np.array([2.0 ** (-8.0 * (i + 1) / n) for i in range(n)], dtype=np.float32))

def causal_short_conv(x, prev, w):
    t = x.shape[1]
    xp = jnp.concatenate([prev.astype(x.dtype), x], axis=1)
    y = xp[:, 0:t] * w[0]
    for i in range(1, GDN_CONV):
        y = y + xp[:, i:i + t] * w[i]
    return jax.nn.silu(y), xp[:, t:]

def gated_delta_rule(q, k, v, g, beta, s0, chunk):
    bsz, t, nh, dk = q.shape
    dv = v.shape[-1]
    n = t // chunk

    def blocks(a):
        a = a.reshape((bsz, n, chunk) + a.shape[2:])
        return jnp.moveaxis(a, 2, 3)

    qc, kc, vc, gc, bc = (blocks(a) for a in (q, k, v, g, beta))
    G = jnp.cumsum(gc, axis=-1)
    i = jnp.arange(chunk)
    lower = i[:, None] >= i[None, :]
    strict = i[:, None] > i[None, :]
    gdiff = G[..., :, None] - G[..., None, :]
    decay = jnp.where(lower, jnp.exp(jnp.where(lower, gdiff, 0.0)), 0.0)
    kk = jnp.einsum('bnhid,bnhjd->bnhij', kc, kc)
    a_mat = jnp.where(strict, bc[..., :, None] * kk * decay, 0.0)
    rhs = jnp.concatenate([vc * bc[..., None], kc * (bc * jnp.exp(G))[..., None]], axis=-1)
    sol = lax.linalg.triangular_solve(a_mat, rhs, left_side=True, lower=True, unit_diagonal=True)
    u, w = sol[..., :dv], sol[..., dv:]
    qk = jnp.where(lower, jnp.einsum('bnhid,bnhjd->bnhij', qc, kc) * decay, 0.0)
    q_dec = qc * jnp.exp(G)[..., None]
    k_dec = kc * jnp.exp(G[..., -1:] - G)[..., None]
    g_end = jnp.exp(G[..., -1])

    def step(s, xs):
        u_c, w_c, qk_c, q_c, k_c, ge = xs
        v_new = u_c - jnp.einsum('bhld,bhdv->bhlv', w_c, s)
        o = jnp.einsum('bhld,bhdv->bhlv', q_c, s) + jnp.einsum('bhij,bhjv->bhiv', qk_c, v_new)
        s = s * ge[..., None, None] + jnp.einsum('bhld,bhlv->bhdv', k_c, v_new)
        return s, o

    xs = tuple(jnp.moveaxis(a, 1, 0) for a in (u, w, qk, q_dec, k_dec, g_end))
    s_fin, o = lax.scan(step, s0, xs)
    o = jnp.transpose(o, (1, 0, 3, 2, 4)).reshape(bsz, t, nh, dv)
    return o, s_fin

def gdn_branch(qkv, z, b_raw, a_raw, conv_prev, s0, conv_w, a_log, dt_bias, norm_g):
    bsz, t, _ = qkv.shape
    c, conv_new = causal_short_conv(qkv, conv_prev, conv_w)
    q, k, v = jnp.split(c, 3, axis=-1)
    hd = (bsz, t, GDN_HEADS, GDN_HEAD_DIM)
    q = l2norm(q.reshape(hd)) * (GDN_HEAD_DIM ** -0.5)
    k = l2norm(k.reshape(hd))
    v = v.reshape(hd).astype(jnp.float32)
    beta = jax.nn.sigmoid(b_raw.astype(jnp.float32))
    g = -jnp.exp(a_log.astype(jnp.float32)) * jax.nn.softplus(a_raw.astype(jnp.float32) + dt_bias.astype(jnp.float32))
    o, s_new = gated_delta_rule(q, k, v, g, beta, s0.astype(jnp.float32), min(CHUNK, t))
    o = rmsnorm(o, norm_g) * jax.nn.silu(z.reshape(hd).astype(jnp.float32))
    return o.reshape(bsz, t, GDN_WIDTH).astype(qkv.dtype), conv_new, s_new.astype(qkv.dtype)

def diff_attend(q, k, v, q_pos, k_pos, lam):
    slopes = alibi_slopes(DIFF_HEADS)
    s = jnp.einsum('bqhmd,bkhmd->bhmqk', q, k).astype(jnp.float32) * (DIFF_HEAD_DIM ** -0.5)
    dist = jnp.abs(q_pos[:, None] - k_pos[None, :]).astype(jnp.float32)
    visible = (k_pos[None, :] // CHUNK) <= (q_pos[:, None] // CHUNK)
    s = jnp.where(visible, s - slopes[:, None, None, None] * dist, -jnp.inf)
    p = jax.nn.softmax(s, axis=-1)
    a = p[:, :, 0] - lam * p[:, :, 1]
    return jnp.einsum('bhqk,bkhe->bqhe', a, v.astype(jnp.float32))

def diff_branch(q, k_rows, v_rows, k_past, v_past, lam):
    bsz, t = q.shape[:2]
    q = q.reshape(bsz, t, DIFF_HEADS, 2, DIFF_HEAD_DIM)
    if k_past is None:
        k = k_rows.reshape(bsz, t, DIFF_HEADS, 2, DIFF_HEAD_DIM)
        pos = jnp.arange(t, dtype=jnp.int32)
        nblk = t // ATTN_BLOCK
        qb = jnp.moveaxis(q.reshape(bsz, nblk, ATTN_BLOCK, DIFF_HEADS, 2, DIFF_HEAD_DIM), 1, 0)
        ob = lax.map(lambda a: diff_attend(a[0], k, v_rows, a[1], pos, lam), (qb, pos.reshape(nblk, ATTN_BLOCK)))
        return jnp.moveaxis(ob, 0, 1).reshape(bsz, t, DIFF_HEADS, DIFF_V_DIM)
    past = k_past.shape[1]
    k = jnp.concatenate([k_past.astype(k_rows.dtype), k_rows], axis=1).reshape(bsz, past + t, DIFF_HEADS, 2, DIFF_HEAD_DIM)
    v = jnp.concatenate([v_past.astype(v_rows.dtype), v_rows], axis=1)
    q_pos = past + jnp.arange(t, dtype=jnp.int32)
    k_pos = jnp.arange(past + t, dtype=jnp.int32)
    return diff_attend(q, k, v, q_pos, k_pos, lam)

def memory_kv(mem, norm_g, w_mk, w_mv):
    hm = rmsnorm(mem, norm_g)
    shp = mem.shape[:2] + (MEM_HEADS, MEM_HEAD_DIM)
    return (hm @ w_mk).reshape(shp), (hm @ w_mv).reshape(shp)

def cross_attend(h, mem_k, mem_v, w_mq, w_mo):
    bsz, t, _ = h.shape
    q = (h @ w_mq).reshape(bsz, t, MEM_HEADS, MEM_HEAD_DIM)
    s = jnp.einsum('bqhd,bkhd->bhqk', q, mem_k.astype(q.dtype)).astype(jnp.float32) * (MEM_HEAD_DIM ** -0.5)
    p = jax.nn.softmax(s, axis=-1)
    o = jnp.einsum('bhqk,bkhd->bqhd', p, mem_v.astype(jnp.float32))
    return o.reshape(bsz, t, D_MODEL).astype(h.dtype) @ w_mo

def peer_block(xb, w_q, sub_keys, u_tab, v_tab):
    n = xb.shape[0]
    q = (xb @ w_q).reshape(n, PEER_HEADS, 2, PEER_HALF)
    s = jnp.einsum('nhpc,hpkc->nhpk', q, sub_keys.astype(q.dtype)).astype(jnp.float32)
    v1, i1 = lax.top_k(s[:, :, 0], PEER_TOPK)
    v2, i2 = lax.top_k(s[:, :, 1], PEER_TOPK)
    cand = (v1[..., :, None] + v2[..., None, :]).reshape(n, PEER_HEADS, PEER_TOPK * PEER_TOPK)
    cidx = (i1[..., :, None] * PEER_N_KEYS + i2[..., None, :]).reshape(n, PEER_HEADS, PEER_TOPK * PEER_TOPK)
    best, sel = lax.top_k(cand, PEER_TOPK)
    eidx = jnp.take_along_axis(cidx, sel, axis=-1)
    gate = jax.nn.softmax(best, axis=-1)
    u = jnp.take(u_tab, eidx, axis=0)
    hid = jax.nn.gelu(jnp.einsum('nd,nhkd->nhk', xb, u.astype(xb.dtype)).astype(jnp.float32))
    coef = (gate * hid).astype(xb.dtype)
    return jnp.einsum('nhk,nhkd->nd', coef, jnp.take(v_tab, eidx, axis=0).astype(xb.dtype))

def peer_ffn(xf, w_q, sub_keys, u_tab, v_tab):
    n = xf.shape[0]
    nb = -(-n // PEER_BLOCK)
    xb = jnp.pad(xf, ((0, nb * PEER_BLOCK - n), (0, 0))).reshape(nb, PEER_BLOCK, D_MODEL)
    out = lax.map(lambda blk: peer_block(blk, w_q, sub_keys, u_tab, v_tab), xb)
    return out.reshape(nb * PEER_BLOCK, D_MODEL)[:n]

def trunk_layer(x, lp, layer, mem_k, mem_v, conv_prev, gdn_state, k_past, v_past):
    bsz, t, _ = x.shape
    h = rmsnorm(x, lp['norm_mix_g'])
    split_pts = [int(c) for c in np.cumsum(IN_SIZES)[:-1]]
    qkv, z, b_raw, a_raw, dq, dk, dv, gate_a, gate_b = jnp.split(h @ lp['w_in'], split_pts, axis=-1)
    o_a, conv_new, s_new = gdn_branch(qkv, z, b_raw, a_raw, conv_prev, gdn_state, lp['gdn_conv_w'],
                                      lp['gdn_a_log'], lp['gdn_dt_bias'], lp['gdn_norm_g'])
    lam_init = 0.8 - 0.6 * math.exp(-0.3 * layer)
    f32 = jnp.float32
    lam = (jnp.exp(jnp.sum(lp['diff_lambda_q1'].astype(f32) * lp['diff_lambda_k1'].astype(f32)))
           - jnp.exp(jnp.sum(lp['diff_lambda_q2'].astype(f32) * lp['diff_lambda_k2'].astype(f32))) + lam_init)
    k_rows = dk.reshape(bsz, t, DIFF_HEADS, 2 * DIFF_HEAD_DIM)
    v_rows = dv.reshape(bsz, t, DIFF_HEADS, DIFF_V_DIM)
    o_b = diff_branch(dq, k_rows, v_rows, k_past, v_past, lam)
    o_b = (rmsnorm(o_b, lp['diff_subln_g']) * (1.0 - lam_init)).reshape(bsz, t, DIFF_WIDTH).astype(x.dtype)
    merged = jax.nn.sigmoid(gate_a) * (o_a @ lp['w_branch_a']) + jax.nn.sigmoid(gate_b) * (o_b @ lp['w_branch_b'])
    x = x + merged @ lp['w_out']
    x = x + cross_attend(rmsnorm(x, lp['norm_cross_g']), mem_k, mem_v, lp['w_mq'], lp['w_mo'])
    hf = rmsnorm(x, lp['norm_ffn_g']).reshape(bsz * t, D_MODEL)
    x = x + peer_ffn(hf, lp['peer_w_q'], lp['peer_sub_keys'], lp['peer_u'], lp['peer_v']).reshape(bsz, t, D_MODEL)
    return x, k_rows, v_rows, s_new, conv_new

def setup_inputs(seed: int = 0) -> dict:
    key = jax.random.key(seed)
    ks = iter(jax.random.split(key, 48))
    f32 = jnp.float32

    def nrm(shape, scale):
        return jax.random.normal(next(ks), shape, f32) * scale

    def gain(shape):
        return 1.0 + 0.02 * jax.random.normal(next(ks), shape, f32)

    L = DEPTH
    inv_d = D_MODEL ** -0.5
    return {
        'x_prompt': nrm((BATCH, SEQ, D_MODEL), 1.0),
        'x_sample': nrm((DEC_BATCH, DEC_SEQ, D_MODEL), 1.0),
        'cache_diff_k': nrm((L, DEC_BATCH, PAST_LEN, DIFF_HEADS, 2 * DIFF_HEAD_DIM), 1.0),
        'cache_diff_v': nrm((L, DEC_BATCH, PAST_LEN, DIFF_HEADS, DIFF_V_DIM), 1.0),
        'state_gdn': nrm((L, DEC_BATCH, GDN_HEADS, GDN_HEAD_DIM, GDN_HEAD_DIM), 0.1),
        'state_conv': nrm((L, DEC_BATCH, GDN_CONV - 1, GDN_CONV_DIM), 1.0),
        'cache_mem_k': nrm((L, DEC_BATCH, MEM_TOKENS, MEM_HEADS, MEM_HEAD_DIM), 1.0),
        'cache_mem_v': nrm((L, DEC_BATCH, MEM_TOKENS, MEM_HEADS, MEM_HEAD_DIM), 1.0),
        'mem_prompt': nrm((BATCH, MEM_TOKENS, D_MODEL), 1.0),
        'norm_mix_g': gain((L, D_MODEL)),
        'w_in': nrm((L, D_MODEL, IN_COLS), inv_d),
        'gdn_conv_w': nrm((L, GDN_CONV, GDN_CONV_DIM), 0.5),
        'gdn_a_log': jnp.log(jax.random.uniform(next(ks), (L, GDN_HEADS), f32, 1.0, 16.0)),
        'gdn_dt_bias': nrm((L, GDN_HEADS), 0.1),
        'gdn_norm_g': gain((L, GDN_HEAD_DIM)),
        'diff_lambda_q1': nrm((L, DIFF_HEAD_DIM), 0.1),
        'diff_lambda_k1': nrm((L, DIFF_HEAD_DIM), 0.1),
        'diff_lambda_q2': nrm((L, DIFF_HEAD_DIM), 0.1),
        'diff_lambda_k2': nrm((L, DIFF_HEAD_DIM), 0.1),
        'diff_subln_g': gain((L, DIFF_V_DIM)),
        'w_branch_a': nrm((L, GDN_WIDTH, D_MODEL), GDN_WIDTH ** -0.5),
        'w_branch_b': nrm((L, DIFF_WIDTH, D_MODEL), DIFF_WIDTH ** -0.5),
        'w_out': nrm((L, D_MODEL, D_MODEL), inv_d),
        'norm_cross_g': gain((L, D_MODEL)),
        'norm_mem_g': gain((L, D_MODEL)),
        'w_mq': nrm((L, D_MODEL, D_MODEL), inv_d),
        'w_mk': nrm((L, D_MODEL, D_MODEL), inv_d),
        'w_mv': nrm((L, D_MODEL, D_MODEL), inv_d),
        'w_mo': nrm((L, D_MODEL, D_MODEL), inv_d),
        'norm_ffn_g': gain((L, D_MODEL)),
        'peer_w_q': nrm((L, D_MODEL, PEER_HEADS * PEER_QUERY_DIM), inv_d),
        'peer_sub_keys': nrm((L, PEER_HEADS, 2, PEER_N_KEYS, PEER_HALF), PEER_HALF ** -0.5),
        'peer_u': nrm((L, PEER_EXPERTS, D_MODEL), inv_d),
        'peer_v': nrm((L, PEER_EXPERTS, D_MODEL), PEER_HEADS ** -0.5),
        'final_norm_g': gain((D_MODEL,)),
    }

def reference(x_prompt, x_sample, cache_diff_k, cache_diff_v, state_gdn, state_conv, cache_mem_k, cache_mem_v,
              mem_prompt, norm_mix_g, w_in, gdn_conv_w, gdn_a_log, gdn_dt_bias, gdn_norm_g,
              diff_lambda_q1, diff_lambda_k1, diff_lambda_q2, diff_lambda_k2, diff_subln_g,
              w_branch_a, w_branch_b, w_out, norm_cross_g, norm_mem_g, w_mq, w_mk, w_mv, w_mo,
              norm_ffn_g, peer_w_q, peer_sub_keys, peer_u, peer_v, final_norm_g):
    yp, ys = x_prompt, x_sample
    pk, pv, ps, pc, pmk, pmv = [], [], [], [], [], []
    sk, sv, ss, sc = [], [], [], []
    for l in range(DEPTH):
        lp = {
            'norm_mix_g': norm_mix_g[l], 'w_in': w_in[l], 'gdn_conv_w': gdn_conv_w[l],
            'gdn_a_log': gdn_a_log[l], 'gdn_dt_bias': gdn_dt_bias[l], 'gdn_norm_g': gdn_norm_g[l],
            'diff_lambda_q1': diff_lambda_q1[l], 'diff_lambda_k1': diff_lambda_k1[l],
            'diff_lambda_q2': diff_lambda_q2[l], 'diff_lambda_k2': diff_lambda_k2[l],
            'diff_subln_g': diff_subln_g[l], 'w_branch_a': w_branch_a[l], 'w_branch_b': w_branch_b[l],
            'w_out': w_out[l], 'norm_cross_g': norm_cross_g[l], 'w_mq': w_mq[l], 'w_mo': w_mo[l],
            'norm_ffn_g': norm_ffn_g[l], 'peer_w_q': peer_w_q[l], 'peer_sub_keys': peer_sub_keys[l],
            'peer_u': peer_u[l], 'peer_v': peer_v[l],
        }
        mem_k, mem_v = memory_kv(mem_prompt, norm_mem_g[l], w_mk[l], w_mv[l])
        conv0 = jnp.zeros((yp.shape[0], GDN_CONV - 1, GDN_CONV_DIM), yp.dtype)
        s0 = jnp.zeros((yp.shape[0], GDN_HEADS, GDN_HEAD_DIM, GDN_HEAD_DIM), yp.dtype)
        yp, k_r, v_r, s_n, c_n = trunk_layer(yp, lp, l, mem_k, mem_v, conv0, s0, None, None)
        pk.append(k_r); pv.append(v_r); ps.append(s_n); pc.append(c_n); pmk.append(mem_k); pmv.append(mem_v)
        ys, k_r, v_r, s_n, c_n = trunk_layer(ys, lp, l, cache_mem_k[l], cache_mem_v[l], state_conv[l],
                                             state_gdn[l], cache_diff_k[l], cache_diff_v[l])
        sk.append(k_r); sv.append(v_r); ss.append(s_n); sc.append(c_n)
    y_prompt = rmsnorm(yp, final_norm_g)
    y_sample = rmsnorm(ys, final_norm_g)
    new_diff_k_prompt = jnp.stack(pk)
    new_diff_v_prompt = jnp.stack(pv)
    new_state_gdn_prompt = jnp.stack(ps)
    new_state_conv_prompt = jnp.stack(pc)
    new_mem_k_prompt = jnp.stack(pmk)
    new_mem_v_prompt = jnp.stack(pmv)
    new_diff_k_sample = jnp.stack(sk)
    new_diff_v_sample = jnp.stack(sv)
    new_state_gdn_sample = jnp.stack(ss)
    new_state_conv_sample = jnp.stack(sc)
    return (y_prompt, y_sample, new_diff_k_prompt, new_diff_v_prompt, new_state_gdn_prompt, new_state_conv_prompt,
            new_mem_k_prompt, new_mem_v_prompt, new_diff_k_sample, new_diff_v_sample, new_state_gdn_sample,
            new_state_conv_sample)


_drawn_inputs = setup_inputs


def setup_inputs(seed=0):
    import zlib

    import numpy as np

    out = dict(_drawn_inputs(seed))
    spreads = {}
    factors = {'state_gdn': 3.063,
     'gdn_dt_bias': 5.814,
     'gdn_norm_g': 4.514,
     'diff_lambda_k2': 2.802,
     'diff_subln_g': 3.29,
     'norm_cross_g': 7.479,
     'norm_mem_g': 2.826,
     'final_norm_g': 8.196,
     'norm_ffn_g': 4.567}
    for name, (base, spread) in spreads.items():
        noise = np.random.default_rng([zlib.crc32(name.encode()), seed]).standard_normal(out[name].shape)
        drawn = base * np.exp(spread * noise) if base else spread * noise
        out[name] = jnp.asarray(drawn.astype(out[name].dtype))
    for name, factor in factors.items():
        out[name] = (out[name] * factor).astype(out[name].dtype)
    return out
```

```python
from contextlib import ExitStack

import numpy as np

import concourse.bass as bass
from concourse import mybir

F32 = mybir.dt.float32
U32 = mybir.dt.uint32
ACT = mybir.ActivationFunctionType
ALU = mybir.AluOpType
AX = mybir.AxisListType

P = 128
D = 2048
KD = D // P
NP_, NS = 512, 32
NT = NP_ + NS
HN = NT // 2
MEM = 256
HEADS = 8
DH = 128
CH = 64
NCH = NP_ // CH
NPAD = NP_ + CH
LEVELS = 6
MH, MD = 4, 512
EPS = 1e-6
NKEY = 128
TOPK = 16
QT = 5
R = 4
GT = 136
LAM_INIT = 0.2

T_MV, T_MK, T_GDN, T_DIFF, T_GATE = 0, 16, 32, 64, 96
T_MERGE, T_OUT, T_MQ, T_MO, T_PQ, T_U = 104, 136, 152, 168, 184, 200
N_STREAM = T_U

CONST = {}
_n = 0
for _name, _w in [("ident", P), ("ones", P), ("upper", CH), ("ge", CH), ("strict", CH), ("nstrict", CH),
                  ("levels", LEVELS * CH), ("iota", P), ("eps", 2), ("slopes", HEADS)]:
    CONST[_name] = (_n, _w)
    _n += _w
N_CONST = _n
SMALL = {}
_n = 0
for _name, _w in [("g_mix", KD), ("g_cross", KD), ("g_mem", KD), ("g_ffn", KD), ("g_final", KD),
                  ("g_gdn", 1), ("g_diff", 1), ("dt_bias", 1), ("a_log", 1), ("lambdas", 4 * 64),
                  ("conv_w", 3 * HEADS * 4), ("conv_state", 3 * HEADS * 3)]:
    SMALL[_name] = (_n, _w)
    _n += _w
N_SMALL = _n


def program(nc, t):
    with ExitStack() as ctx:
        def sem(name):
            return ctx.enter_context(nc.semaphore(name))

        ring = ctx.enter_context(nc.sbuf_tensor("ring", [P, R, D], F32))
        H = ctx.enter_context(nc.sbuf_tensor("H", [P, KD, NT], F32))
        BIG = 2 * KD * NT
        OAB_N = HEADS * NPAD + HEADS * NT
        arena = ctx.enter_context(nc.sbuf_tensor("arena", [P, BIG + OAB_N], F32))
        TMP_N = 7680
        tmp = ctx.enter_context(nc.sbuf_tensor("tmp", [P, TMP_N], F32))
        const = ctx.enter_context(nc.sbuf_tensor("const", [P, N_CONST], F32))
        small = ctx.enter_context(nc.sbuf_tensor("small", [P, N_SMALL], F32))
        lamb = ctx.enter_context(nc.sbuf_tensor("lamb", [P, 8], F32))
        psum = ctx.enter_context(nc.psum_tensor("psum", [P, 8, 512], F32))

        def view(buf, start, *shape):
            n = int(np.prod(shape))
            v = buf[:, start:start + n]
            if len(shape) == 2:
                v = v.rearrange("p (a b) -> p a b", a=shape[0])
            if len(shape) == 3:
                v = v.rearrange("p (a b c) -> p a b c", a=shape[0], b=shape[1])
            return v, start + n

        def cst(name, rows=P):
            o, w = CONST[name]
            return const[0:rows, o:o + w]

        def sml(name):
            o, w = SMALL[name]
            return small[:, o:o + w]

        ident, ones, iota = cst("ident"), cst("ones"), cst("iota")
        levels = cst("levels", CH).rearrange("p (l c) -> p l c", l=LEVELS)
        eps = cst("eps")[:, 0:1]

        acc = [psum[:, 2 * b:2 * b + 2, 0:HN] for b in range(2)]
        aux = [psum[:, 4 + 2 * b:6 + 2 * b, 0:HN] for b in range(2)]

        X, _ = view(arena, 0, KD, NT)
        M, _ = view(arena, KD * NT, KD, NT)
        QKV, qkv_end = view(arena, 0, 3 * HEADS, NPAD)
        OA, _ = view(arena, BIG, HEADS, NPAD)
        OB, _ = view(arena, BIG + HEADS * NPAD, HEADS, NT)
        OC, _ = view(arena, BIG, KD, NT)
        memT, _ = view(arena, BIG, KD, MEM)
        hmT, _ = view(arena, KD * NT, KD, MEM)
        stage = [view(tmp, 2000 + 1024 * b, 2, 512)[0] for b in range(2)]

        w_full = [sem(f"w_full{s}") for s in range(R)]
        tile_done = sem("tile_done")
        acc_free = sem("acc_free")
        consts_in, x_in, mem_in = sem("consts_in"), sem("x_in"), sem("mem_in")
        zeroed = sem("zeroed")
        sq_ready, ss_ready = sem("sq_ready"), sem("ss_ready")
        root_ready, norm_ready = sem("root_ready"), sem("norm_ready")
        outs = sem("outs")
        pe_turn = sem("pe_turn")
        staged, stage_out = sem("staged"), [sem("stage_out0"), sem("stage_out1")]
        mv_full, mv_free = sem("mv_full"), sem("mv_free")

        root, _ = view(tmp, TMP_N - 2 * HN, 2, HN)
        NORMS = ["mem", "mix", "cross", "ffn", "final"]

        def norm_halves(name):
            return [(0, MEM)] if name == "mem" else [(0, HN), (HN, HN)]

        def norm_act(act, name, src, dst):
            m = NORMS.index(name)
            for c in range(4):
                nc.scalar.activation(dst[:, 4 * c:4 * c + 4, :], src[:, 4 * c:4 * c + 4, :],
                                     ACT.Square).then_inc(sq_ready, 1)
            act.wait_ge(ss_ready, m + 1)
            halves = norm_halves(name)
            nc.scalar.activation(root[:, 0:len(halves), 0:halves[0][1]],
                                 psum[:, 4:4 + len(halves), 0:halves[0][1]],
                                 ACT.Sqrt, bias=eps, scale=1.0 / D).then_inc(root_ready, 1)

        def norm_pe(pe, name, dst):
            m = NORMS.index(name)
            for c in range(4):
                pe.wait_ge(sq_ready, 4 * m + c + 1)
                for k in range(4 * c, 4 * c + 4):
                    for b, (o, w) in enumerate(norm_halves(name)):
                        mm = nc.tensor.matmul(psum[:, 4 + b, 0:w], ones, dst[:, k, o:o + w],
                                              start=(k == 0), stop=(k == KD - 1))
            mm.then_inc(ss_ready, 1)

        def norm_dve(dve, name, src, dst, gain):
            m = NORMS.index(name)
            dve.wait_ge(root_ready, m + 1)
            halves = norm_halves(name)
            w = halves[0][1]
            rt = root[:, 0:len(halves), 0:w]
            nc.vector.reciprocal(rt, rt)
            dve.drain()
            for k in range(KD):
                mul = nc.vector.scalar_tensor_tensor(
                    out=dst[:, k, :].rearrange("p (h n) -> p h n", n=w),
                    in0=src[:, k, :].rearrange("p (h n) -> p h n", n=w),
                    scalar=gain[:, k:k + 1], in1=rt, op0=ALU.mult, op1=ALU.mult)
            mul.then_inc(norm_ready, 1)

        def freed(tile):
            return tile - 2 - T_MK + 1

        def gemm_tile(pe, tile, src):
            if isinstance(tile, tuple):
                i, per, off = tile
                full, free, k0 = i * (16 * per // R) + 16 * (off // R + 1), i * per + freed(off), off
            else:
                full, free, k0 = 16 * (tile // R + 1), freed(tile), tile
            pe.wait_ge(w_full[k0 % R], full)
            pe.wait_ge(acc_free, free)
            for k in range(KD):
                for b in range(2):
                    mm = nc.tensor.matmul(acc[k0 % 2][:, b, :], ring[:, k0 % R, k * P:(k + 1) * P],
                                          src[:, k, b * HN:(b + 1) * HN], start=(k == 0), stop=(k == KD - 1))
            mm.then_inc(tile_done, 1)

        def done(off, i=None, per=None):
            return off + 1 if i is None else i * per + (off + 1)

        xp, e = view(tmp, 0, 3, 3 + NP_ + 3 + NS)
        yc, e = view(tmp, e, 3, NP_ + 3 + NS)
        cq, e = view(tmp, e, 2, NT)
        sqk, e = view(tmp, e, 2, NT)
        rqk = yc
        assert e <= TMP_N
        a_end = qkv_end
        conv_out, a_end = view(arena, a_end, HEADS, 18)
        BG = arena[0:64, a_end:a_end + NPAD]
        a_end += NPAD
        bgt = arena[0:64, a_end:a_end + NPAD]
        wba, e = view(arena, a_end + NPAD, KD, 64)
        assert e <= BIG
        raw_ready, conv_done, qk_sq, qk_ss = sem("raw_ready"), sem("conv_done"), sem("qk_sq"), sem("qk_ss")
        qk_root, qk_done = sem("qk_root"), sem("qk_done")
        ba_full, ba_free, ba_parts, ba_done, ba_in = (sem("ba_full"), sem("ba_free"), sem("ba_parts"),
                                                      sem("ba_done"), sem("ba_in"))

        e = a_end
        Sp, e = view(arena, e, HEADS, DH)
        Ss, e = view(arena, e, HEADS, DH)
        Vc, e = view(arena, e, HEADS, CH)
        assert e <= BIG
        e = BIG + HEADS * NPAD
        Kt, e = view(arena, e, HEADS, DH)
        Vt, e = view(arena, e, HEADS, DH)
        VN, e = view(arena, e, HEADS, DH)
        kd, e = view(arena, e, HEADS, DH)
        assert e <= BIG + OAB_N
        e = 0
        blk = {}
        for name in ("Kc", "Qc", "gU", "Dd", "ET", "ES", "EG", "A", "Bl", "kg", "qd", "QKT", "R"):
            blk[name], e = view(tmp, e, HEADS, CH)
        Tt, e = view(tmp, e, HEADS, CH)
        bc, e = tmp[0:64, e:e + CH], e + CH
        bg, e = tmp[0:64, e:e + CH], e + CH
        gcol, e = tmp[0:64, e:e + 8], e + 8
        ek, e = tmp[0:64, e:e + 8], e + 8
        assert e <= TMP_N, e
        Kc, Qc, gU, Dd, ET, ES, EG, A, Bl, kg, qd, QKT, Rt = (blk[n] for n in (
            "Kc", "Qc", "gU", "Dd", "ET", "ES", "EG", "A", "Bl", "kg", "qd", "QKT", "R"))
        XS, oS, sqo, rto = ES, ET, gU, Dd
        names = ("c_qb c_kv p_bg d_gu p_kt p_vt a_kvt p_kk p_g d_dd a_exp d_a p_x a_x p_rt d_r p_ks d_rr "
                 "p_vn a_vn p_o p_s d_s a_o p_oss a_rto d_o").split()
        s = {n: sem("gdn_" + n) for n in names}
        state_in = sem("state_in")
        b8 = [psum[:, i, :] for i in range(8)]

        def hc(ap, w=CH):
            return ap.rearrange("p (h c) -> p h c", c=w)

        def two(b, rows=P):
            return psum[0:rows, b:b + 2, :].rearrange("p b (h c) -> p (b h) c", c=DH)

        e = 0
        ndist, e = view(arena, e, 4, NP_)
        ndist_s, e = view(arena, e, 1, NT)
        qh, e = view(arena, e, 1, NT)
        kh, e = view(arena, e, 1, NT)
        vh, e = view(arena, e, 1, NT)
        kc, e = view(arena, e, 1, NP_)
        vc, e = view(arena, e, 4, DH)
        assert e <= KD * NT
        vt, e = view(tmp, 0, QT, DH)
        sc, e = view(tmp, e, 2, NT)
        pr, e = view(tmp, e, 1, NT)
        aT, e = view(tmp, e, 4, P)
        ob, e = view(tmp, e, 1, NT)
        osq, e = view(tmp, e, 1, NT)
        ort, e = view(tmp, e, 2, HN)
        st, e = view(tmp, e, 1, 16)
        assert e <= TMP_N
        qh, kh, vh, kc, pr, ob, osq, st = (v[:, 0, :] for v in (qh, kh, vh, kc, pr, ob, osq, st))
        ndist_s = ndist_s[:, 0, :]
        mx, zz, rz = st[:, 0:2], st[:, 2:4], st[:, 4:6]
        g_diff8 = lamb[:, 5:6]
        lam, nlam = lamb[:, 3:4], lamb[:, 4:5]
        at = {n: sem("att_" + n) for n in
              "dist_in qkv cache_in rows_out pvt vt s m e a pT aT o obs oss rt done".split()}
        lam_parts, lam_exp = sem("lam_parts"), sem("lam_exp")

        sgb, e = view(tmp, 0, 2, HN)
        t1, e = view(tmp, e, 2, HN)
        gates_ready, merged = sem("gates_ready"), sem("merged")
        x_again = sem("x_again")
        x_done = sem("x_done")

        def hregion(start, a, b):
            return view(H[:, :, :].rearrange("p a b -> p (a b)"), start, a, b)
        mkp, e = hregion(0, 4, MEM)
        mks, e = hregion(e, 4, MEM)
        mvp, e = hregion(e, 2, MD)
        mvs, e = hregion(e, 2, MD)
        qst, e = view(tmp, 0, 4, NT)
        pm, e = view(tmp, e, 4, MEM)
        pms, e = view(tmp, e, 1, MEM)
        pmT, e = view(tmp, e, 2, NP_)
        pmTs, e = view(tmp, e, 2, NS)
        mst, e = view(tmp, e, 1, 16)
        assert e <= TMP_N
        pms, mst = pms[:, 0, :], mst[:, 0, :]
        ca = {n: sem("cross_" + n) for n in
              "qfree in s m e p pT T o oev".split()}
        ca_kv = ca["in"]

        qps, e = view(tmp, 0, 4, NT)
        SC, e = view(arena, KD * NT, QT, 2 * HEADS * NKEY)
        skT, e = view(arena, e, 2 * HEADS, NKEY)
        eqb, e = view(arena, e, P, TOPK)
        work, e = view(arena, e, 2 * HEADS, NKEY)
        assert e <= BIG + OAB_N, e
        sct, e = view(tmp, 0, 2 * HEADS, NKEY)
        slotT, e = view(tmp, e, 3, QT * P)
        tv, e = view(tmp, e, 2 * HEADS, TOPK)
        tif, e = view(tmp, e, 2 * HEADS, TOPK)
        bestv, e = view(tmp, e, HEADS, TOPK)
        abf, e = view(tmp, e, 2, P)
        slots, e = view(tmp, e, 3, P)
        zs, e = view(tmp, e, 1, 8)
        assert e <= TMP_N, e
        tiu = ctx.enter_context(nc.sbuf_tensor("tiu", [P, 2 * HEADS, TOPK], U32))
        selu = ctx.enter_context(nc.sbuf_tensor("selu", [P, 3, HEADS, TOPK], U32))
        pk = {n: sem("peer_" + n) for n in
              "keys_in qs s sev top gexp sl slT slTe oh g gev stored gin".split()}
        oh2, e = view(tmp, 0, 4, P)
        oh1, e = view(tmp, e, 4, P)
        oh2b, e = view(tmp, e, 4, P)
        oh1b, e = view(tmp, e, 4, P)
        OH2, OH1 = [oh2, oh2b], [oh1, oh1b]
        assert e <= 2048
        Gs, _ = view(arena, KD * NT, P, GT)

        vring, _ = view(arena, BIG, R, D)
        assert R * D <= OAB_N
        coef = [view(arena, KD * NT + b * 4 * NT, 4, NT)[0] for b in range(2)]
        gat = [view(arena, KD * NT + (2 + b) * 4 * NT, 4, NT)[0] for b in range(2)]
        hid, _ = view(tmp, 0, 2, NT)
        v_full, g_full = sem("v_full"), [sem("g_full0"), sem("g_full1")]
        hid_ready, hid_free, coef_ready, v_done = sem("hid_ready"), sem("hid_free"), sem("coef_ready"), sem("v_done")
        y_full, y_free = sem("y_full"), sem("y_free")
        y_out = sem("y_out")
        NG = NKEY // 4

        block = ctx.enter_context(nc.Block())

        @block.sync
        def _(sp):
            sp.dma_start(const[:, :], t["consts"]).then_inc(consts_in, 16)
            sp.dma_start(small[:, :], t["small"]).then_inc(consts_in, 16)
            sp.dma_start(memT, t["memT"]).then_inc(mem_in, 16)
            for k in range(R):
                sp.dma_start(ring[:, k, :], t["weights"][k]).then_inc(w_full[k], 16)
            sp.dma_start(X, t["xT"]).then_inc(x_in, 16)
            sp.dma_start(wba, t["w_ba"]).then_inc(ba_in, 16)
            with sp.Fori(1, N_STREAM // R) as i:
                for k in range(R):
                    src = t["weights"][bass.ds(i * R + k, 1)].rearrange("o p n -> p (o n)")
                    sp.wait_ge(tile_done, i * R + (k - R + 1))
                    sp.dma_start(ring[:, k, :], src).then_inc(w_full[k], 16)

            def load_u(group, reg=None):
                for k in range(R):
                    src = t["uT"][group * R + k] if reg is None else \
                        t["uT"][bass.ds(reg * R + (group * R + k), 1)].rearrange("o p n -> p (o n)")
                    n = T_U + (group - 1) * R + k + 1
                    sp.wait_ge(tile_done, n if reg is None else reg * R + n)
                    sp.dma_start(ring[:, k, :], src).then_inc(w_full[k], 16)

            def load_v(group, reg=None):
                src = t["v"][group * R:(group + 1) * R] if reg is None else \
                    t["v"][bass.ds(reg * R + group * R, R)]
                if reg is not None:
                    sp.wait_ge(v_done, reg + (2 + group))
                sp.dma_start(vring, src.rearrange("r p n -> p r n")).then_inc(v_full, 16)

            load_u(0)
            sp.wait_ge(pk["stored"], 32 * (NT // GT))
            load_v(0)
            load_u(1)
            with sp.Fori(0, NG - 2) as g:
                load_u(2, g)
                load_v(1, g)
            sp.wait_ge(v_done, 2 + NG - 1)
            sp.dma_start(vring, t["v"][(NG - 1) * R:NG * R].rearrange("r p n -> p r n")).then_inc(v_full, 16)
            sp.wait_ge(norm_ready, len(NORMS))
            sp.dma_start(t["y"], H[:, :, :]).then_inc(y_out, 16)
            sp.wait_ge(y_out, 16)

        @block.gpsimd
        def _(pool):
            nc.gpsimd.memset(xp[:, :, 0:3], 0.0).then_inc(zeroed, 1)
            for g in range(4):
                pool.wait_ge(staged, g + 1)
                pool.dma_start(t["mem_v"][:, :, g * 512:(g + 1) * 512], stage[g % 2]).then_inc(stage_out[g % 2], 16)
            for k in range(KD):
                pool.wait_ge(staged, 4 + k + 1)
                pool.dma_start(t["mem_k"][k], stage[k % 2][:, 0, 0:MEM]).then_inc(stage_out[k % 2], 16)
            pool.wait_ge(norm_ready, 2)
            nc.gpsimd.memset(QKV[:, :, NT:NPAD], 0.0)
            nc.gpsimd.memset(OA[:, :, NT:NPAD], 0.0)
            nc.gpsimd.memset(BG, 0.0)
            pool.drain().then_inc(zeroed, 1)
            pool.wait_ge(ba_done, 1)
            nc.gpsimd.memset(Sp, 0.0).then_inc(zeroed, 1)
            pool.dma_start(Ss, t["state_in"]).then_inc(state_in, 16)
            pool.wait_ge(conv_done, 3 * HEADS)
            pool.wait_ge(qk_done, HEADS)
            pool.dma_start(t["conv_state"], conv_out).then_inc(outs, 16)
            pool.wait_ge(s["d_s"], NCH)
            pool.dma_start(t["state_p"], Sp).then_inc(outs, 16)
            pool.wait_ge(s["d_s"], NCH + 1)
            pool.dma_start(t["state_s"], Ss).then_inc(outs, 16)
            pool.wait_ge(s["d_o"], NCH + 1)
            pool.wait_ge(outs, 48)
            pool.dma_start(ndist, t["ndist"]).then_inc(at["dist_in"], 16)
            pool.dma_start(ndist_s[0:NS, :], t["ndist_s"]).then_inc(at["dist_in"], 16)
            pool.dma_start(kc, t["cache_k"][0]).then_inc(at["cache_in"], 16)
            pool.dma_start(vc, t["cache_v"][0]).then_inc(at["cache_in"], 16)

            def rows_out(h, k_dst, v_dst):
                pool.wait_ge(at["qkv"], h * 3 + 3)
                pool.dma_start(k_dst, kh).then_inc(at["rows_out"], 16)
                pool.dma_start(v_dst, vh).then_inc(at["rows_out"], 16)

            with pool.Fori(0, HEADS - 1) as h:
                k_dst = t["k_rows"][bass.ds(h, 1)].rearrange("o p n -> p (o n)")
                v_dst = t["v_rows"][bass.ds(h, 1)].rearrange("o p n -> p (o n)")
                k_src = t["cache_k"][bass.ds(h + 1, 1)].rearrange("o p n -> p (o n)")
                v_src = t["cache_v"][bass.ds(h + 1, 1)].rearrange("o p b n -> p (o b) n")
                rows_out(h, k_dst, v_dst)
                pool.wait_ge(at["o"], h * 5 + 5)
                pool.dma_start(kc, k_src).then_inc(at["cache_in"], 16)
                pool.dma_start(vc, v_src).then_inc(at["cache_in"], 16)
            rows_out(HEADS - 1, t["k_rows"][HEADS - 1], t["v_rows"][HEADS - 1])
            pool.wait_ge(at["done"], HEADS)
            pool.wait_ge(at["rows_out"], 32 * HEADS)
            pool.dma_start(X, t["xT"]).then_inc(x_again, 16)
            for b in range(2):
                pool.wait_ge(stage_out[b], 16 * 10)
            with pool.Fori(0, MH) as h:
                srcs = [t["mem_k"][bass.ds(h * 4, 4)].rearrange("c p n -> p c n"),
                        t["cmem_k"][bass.ds(h * 4, 4)].rearrange("c p n -> p c n"),
                        t["mem_v"][:, :, bass.ds(h * MD, MD)],
                        t["cmem_v"][:, :, bass.ds(h * MD, MD)]]
                pool.wait_ge(ca["qfree"], h + 1)
                for dst, src in zip((mkp, mks, mvp, mvs), srcs):
                    pool.dma_start(dst, src).then_inc(ca_kv, 16)
            pool.wait_ge(x_done, 2)
            pool.dma_start(skT, t["sub_keys"]).then_inc(pk["keys_in"], 16)
            with pool.Fori(0, NT // GT) as g:
                dsts = [t["gates"][:, 64 * j:64 * j + 64, bass.ds(g * GT, GT)] for j in range(2)]
                pool.wait_ge(pk["gev"], g * (GT // 4) + (GT // 4 + 2))
                for j in range(2):
                    pool.dma_start(dsts[j], Gs[:, 64 * j:64 * j + 64, :]).then_inc(pk["stored"], 16)
            pool.wait_ge(pk["stored"], 32 * (NT // GT))
            for g in range(2):
                pool.dma_start(gat[g], t["gates"][:, 4 * g:4 * g + 4, :]).then_inc(g_full[g], 16)
            with pool.Fori(0, NG // 2 - 1) as i:
                for b in range(2):
                    src = t["gates"][:, bass.ds(i * 8 + (8 + 4 * b), 4), :]
                    pool.wait_ge(coef_ready, i * 8 + 4 * (b + 1))
                    pool.dma_start(gat[b], src).then_inc(g_full[b], 16)

        @block.tensor
        def _(pe):
            pe.wait_ge(consts_in, 32)

            def wait_first(semaphore, value):
                pe.wait_ge(semaphore, value)
                pe.sem_inc(pe_turn, 1)

            norm_pe(pe, "mem", hmT)
            pe.wait_ge(norm_ready, 1)
            for g in range(4):
                if g >= 2:
                    pe.wait_ge(mv_free, g - 1)
                for kq in range(4):
                    tile = T_MV + 4 * g + kq
                    pe.wait_ge(w_full[tile % R], 16 * (tile // R + 1))
                    for k in range(4):
                        for m in range(2):
                            mm = nc.tensor.matmul(psum[:, 2 * (g % 2) + m, :],
                                                  hmT[:, 4 * kq + k, m * P:(m + 1) * P],
                                                  ring[:, tile % R, k * 512:(k + 1) * 512],
                                                  start=(kq == 0 and k == 0), stop=(kq == 3 and k == 3))
                    mm.then_inc(tile_done, 1)
            pe.wait_ge(mv_free, 4)
            for n in range(KD):
                tile = T_MK + n
                pe.wait_ge(w_full[tile % R], 16 * (tile // R + 1))
                if n >= 2:
                    pe.wait_ge(acc_free, n - 1)
                for k in range(KD):
                    mm = nc.tensor.matmul(psum[:, 2 * (n % 2), 0:MEM], ring[:, tile % R, k * P:(k + 1) * P],
                                          hmT[:, k, :], start=(k == 0), stop=(k == KD - 1))
                mm.then_inc(tile_done, 1)

            norm_pe(pe, "mix", H)
            pe.wait_ge(norm_ready, 2)
            pe.wait_ge(ba_in, 16)
            for k in range(KD):
                for b in range(2):
                    mm = nc.tensor.matmul(psum[0:64, 6 + b, 0:HN], wba[:, k, :], H[:, k, b * HN:(b + 1) * HN],
                                          start=(k == 0), stop=(k == KD - 1))
            mm.then_inc(ba_full, 1)
            pe.wait_ge(ba_free, 1)
            with pe.Fori(0, HEADS) as i:
                for j in range(4):
                    gemm_tile(pe, (i, 4, T_GDN + j), H)
                pe.wait_ge(qk_sq, i * 2 + 2)
                for j in range(2):
                    for b in range(2):
                        mm = nc.tensor.matmul(aux[j][:, b, :], ones, sqk[:, j, b * HN:(b + 1) * HN],
                                              start=True, stop=True)
                mm.then_inc(qk_ss, 1)

            def gdn_block(c, S):
                one = c + 1
                wait_first(s["c_qb"], one)
                nc.tensor.transpose(b8[0][0:64, 0:64], bc, ident[0:64, 0:64]).then_inc(s["p_bg"], 1)
                wait_first(s["c_kv"], one)
                for h in range(HEADS):
                    mm = nc.tensor.transpose(two(4, CH)[:, h, :], Kc[:, h, :], ident)
                mm.then_inc(s["p_kt"], 1)
                for h in range(HEADS):
                    mm = nc.tensor.transpose(two(6, CH)[:, h, :], Vc[:, h, :], ident)
                mm.then_inc(s["p_vt"], 1)
                for h in range(HEADS):
                    nc.tensor.matmul(hc(b8[2])[0:CH, h, :], Kc[:, h, :], Kc[:, h, :], start=True, stop=True)
                    mm = nc.tensor.matmul(hc(b8[3])[0:CH, h, :], Kc[:, h, :], Qc[:, h, :], start=True, stop=True)
                mm.then_inc(s["p_kk"], 1)
                wait_first(s["d_gu"], one)
                nc.tensor.matmul(b8[0][0:CH, 64:72], cst("upper", CH), bg[:, 32:40], start=True, stop=True)
                nc.tensor.matmul(b8[1], ones[0:CH, :], gU[0:CH, :, :], start=True, stop=True)\
                    .then_inc(s["p_g"], 1)
                wait_first(s["d_a"], one)
                for h in range(HEADS):
                    mm = nc.tensor.matmul(hc(b8[0])[0:CH, h, :], Bl[0:CH, h, :], ident[0:CH, 0:CH],
                                          start=True, stop=True)
                mm.then_inc(s["p_x"], 1)
                for lv in range(1, LEVELS):
                    wait_first(s["d_r"], c * LEVELS + lv)
                    for h in range(HEADS):
                        mm = nc.tensor.matmul(hc(b8[0])[0:CH, h, :], Bl[0:CH, h, :], Rt[0:CH, h, :],
                                              start=True, stop=True)
                    mm.then_inc(s["p_x"], 1)
                    wait_first(s["a_x"], c * (LEVELS - 1) + lv)
                    for h in range(HEADS):
                        nc.tensor.matmul(hc(b8[1])[0:CH, h, :], Tt[0:CH, h, :], XS[0:CH, h, :],
                                         start=True, stop=True)
                    for h in range(HEADS):
                        mm = nc.tensor.matmul(hc(b8[2])[0:CH, h, :], XS[0:CH, h, :], Tt[0:CH, h, :],
                                              start=True, stop=True)
                    mm.then_inc(s["p_rt"], 1)
                pe.wait_ge(s["a_kvt"], c * 2 + 2)
                for h in range(HEADS):
                    mm = nc.tensor.matmul(two(4, CH)[:, h, :], kg[:, h, :], S[:, h, :], start=True, stop=True)
                mm.then_inc(s["p_ks"], 1)
                wait_first(s["d_rr"], one)
                for h in range(HEADS):
                    mm = nc.tensor.matmul(two(6, CH)[:, h, :], Rt[0:CH, h, :], Vt[0:CH, h, :],
                                          start=True, stop=True)
                mm.then_inc(s["p_vn"], 1)
                wait_first(s["a_vn"], one)
                for h in range(HEADS):
                    nc.tensor.matmul(hc(b8[3])[:, h, :], S[:, h, :], qd[:, h, :], start=True, stop=False)
                    mm = nc.tensor.matmul(hc(b8[3])[:, h, :], VN[0:CH, h, :], QKT[0:CH, h, :],
                                          start=False, stop=True)
                mm.then_inc(s["p_o"], 1)
                for h in range(HEADS):
                    mm = nc.tensor.matmul(two(4)[:, h, :], kd[0:CH, h, :], VN[0:CH, h, :],
                                          start=True, stop=True)
                mm.then_inc(s["p_s"], 1)
                pe.wait_ge(s["a_o"], one)
                nc.tensor.matmul(b8[1], ones, sqo, start=True, stop=True).then_inc(s["p_oss"], 1)

            pe.wait_ge(qk_done, HEADS)
            pe.wait_ge(acc_free, freed(T_DIFF + 1))
            with pe.Fori(0, NCH) as c:
                gdn_block(c, Sp)
            pe.wait_ge(state_in, 16)
            gdn_block(NCH, Ss)
            pe.wait_ge(s["d_o"], NCH + 1)

            with pe.Fori(0, HEADS) as h:
                for j in range(4):
                    gemm_tile(pe, (h, 4, T_DIFF + j), H)
                pe.wait_ge(at["qkv"], h * 3 + 3)
                for b in range(4):
                    nc.tensor.transpose(psum[:, 6, b * P:(b + 1) * P], vh[:, b * P:(b + 1) * P], ident)
                nc.tensor.transpose(psum[0:NS, 7, 0:P], vh[:, NP_:NT], ident).then_inc(at["pvt"], 1)
                for q in range(QT):
                    if q == 0:
                        wait_first(at["vt"], h + 1)
                    else:
                        wait_first(at["m"], h * 10 + 2 * q)
                    if q == 4:
                        wait_first(at["cache_in"], h * 32 + 32)
                        wait_first(at["obs"], h * 2 + 1)
                    for m in range(2):
                        r = slice(64 * m, 64 * m + 64)
                        if q < 4:
                            mm = nc.tensor.matmul(psum[:, 4 + m, 0:P * (q + 1)], qh[r, q * P:(q + 1) * P],
                                                  kh[r, 0:P * (q + 1)], start=True, stop=True)
                        else:
                            nc.tensor.matmul(psum[0:NS, 4 + m, :], qh[r, NP_:NT], kc[r, :], start=True, stop=True)
                            mm = nc.tensor.matmul(psum[0:NS, 7 - m, 64 * m:64 * m + NS], qh[r, NP_:NT],
                                                  kh[r, NP_:NT], start=True, stop=True)
                        mm.then_inc(at["s"], 1)
                    wait_first(at["a"], h * 5 + q + 1)
                    if q < 4:
                        for b in range(q + 1):
                            mm = nc.tensor.transpose(psum[:, 6, b * P:(b + 1) * P], pr[:, b * P:(b + 1) * P], ident)
                    else:
                        nc.tensor.transpose(psum[0:NS, 6, P:P + NS], pr[0:NS, NP_:NT], ident[0:NS, 0:NS])
                        for b in range(4):
                            mm = nc.tensor.transpose(psum[:, 6, b * NS:(b + 1) * NS], pr[0:NS, b * P:(b + 1) * P],
                                                     ident[0:NS, 0:NS])
                    mm.then_inc(at["pT"], 1)
                    wait_first(at["aT"], h * 5 + q + 1)
                    if q < 4:
                        for b in range(q + 1):
                            mm = nc.tensor.matmul(psum[:, 7, q * P:(q + 1) * P], vt[:, b, :], aT[:, b, :],
                                                  start=(b == 0), stop=(b == q))
                    else:
                        for b in range(4):
                            nc.tensor.matmul(psum[:, 7, 0:NS], vc[:, b, :], aT[:, 0, b * NS:(b + 1) * NS],
                                             start=(b == 0), stop=False)
                        mm = nc.tensor.matmul(psum[:, 7, 0:NS], vt[0:NS, 4, :], aT[0:NS, 1, 0:NS],
                                              start=False, stop=True)
                    mm.then_inc(at["o"], 1)
                wait_first(at["obs"], h * 2 + 2)
                for b in range(2):
                    mm = nc.tensor.matmul(psum[:, 4 + b, 0:HN], ones, osq[:, b * HN:(b + 1) * HN],
                                          start=True, stop=True)
                mm.then_inc(at["oss"], 1)
            pe.wait_ge(at["done"], HEADS)

            with pe.Fori(0, 2) as i:
                for k in range(4):
                    gemm_tile(pe, (i, 4, T_GATE + k), H)
            with pe.Fori(0, 8) as i:
                for d in range(2):
                    gemm_tile(pe, (i, 4, T_MERGE + 2 * d), H)
                    tile = T_MERGE + 2 * d + 1
                    pe.wait_ge(w_full[tile % R], i * 16 + 16 * (tile // R + 1))
                    pe.wait_ge(acc_free, i * 4 + freed(tile))
                    pe.wait_ge(merged, i * 2 + (d + 1))
                    for k in range(HEADS):
                        for b in range(2):
                            nc.tensor.matmul(acc[1][:, b, :], ring[:, tile % R, k * P:(k + 1) * P],
                                             OA[:, k, b * HN:(b + 1) * HN],
                                             start=(k == 0), stop=(k == HEADS - 1))
                    for k in range(HEADS):
                        for b in range(2):
                            mm = nc.tensor.matmul(aux[d % 2][:, b, :],
                                                  ring[:, tile % R, (HEADS + k) * P:(HEADS + k + 1) * P],
                                                  OB[:, k, b * HN:(b + 1) * HN],
                                                  start=(k == 0), stop=(k == HEADS - 1))
                    mm.then_inc(tile_done, 1)
            pe.wait_ge(merged, 17)
            with pe.Fori(0, 4) as i:
                for k in range(4):
                    gemm_tile(pe, (i, 4, T_OUT + k), M)
            norm_pe(pe, "cross", H)
            pe.wait_ge(norm_ready, 3)

            with pe.Fori(0, 4) as i:
                for k in range(4):
                    gemm_tile(pe, (i, 4, T_MQ + k), H)
            pe.drain().then_inc(ca["qfree"], 1)
            with pe.Fori(0, MH) as h:
                pe.wait_ge(ca_kv, h * 64 + 64)
                pe.wait_ge(ca["T"], h * 3 + 1)
                for q in range(4):
                    for k in range(4):
                        mm = nc.tensor.matmul(psum[:, 4 + q // 2, (q % 2) * MEM:(q % 2 + 1) * MEM],
                                              qst[:, k, q * P:(q + 1) * P], mkp[:, k, :],
                                              start=(k == 0), stop=(k == 3))
                mm.then_inc(ca["s"], 1)
                for k in range(4):
                    mm = nc.tensor.matmul(psum[0:NS, 6, 0:MEM], qst[:, k, NP_:NT], mks[:, k, :],
                                          start=(k == 0), stop=(k == 3))
                mm.then_inc(ca["s"], 1)
                wait_first(ca["p"], h * 2 + 1)
                for b in range(2):
                    for q in range(4):
                        mm = nc.tensor.transpose(psum[:, 4 + b, q * P:(q + 1) * P], pm[:, q, b * P:(b + 1) * P], ident)
                mm.then_inc(ca["pT"], 1)
                wait_first(ca["p"], h * 2 + 2)
                for b in range(2):
                    mm = nc.tensor.transpose(psum[:, 6, b * NS:(b + 1) * NS], pms[0:NS, b * P:(b + 1) * P],
                                             ident[0:NS, 0:NS])
                mm.then_inc(ca["pT"], 1)
                pe.wait_ge(ca["T"], h * 3 + 3)
                for k in range(4):
                    pe.wait_ge(ca["oev"], h * 4 + (k + 1))
                    for b in range(2):
                        nc.tensor.matmul(psum[:, 2 * (k % 2), :], mvp[:, b, k * P:(k + 1) * P], pmT[:, b, :],
                                         start=(b == 0), stop=(b == 1))
                    for b in range(2):
                        mm = nc.tensor.matmul(psum[:, 2 * (k % 2) + 1, 0:NS], mvs[:, b, k * P:(k + 1) * P],
                                              pmTs[:, b, :], start=(b == 0), stop=(b == 1))
                    mm.then_inc(ca["o"], 1)
                pe.drain().then_inc(ca["qfree"], 1)
            pe.wait_ge(ca["oev"], 2 + 16)
            with pe.Fori(0, 4) as i:
                for k in range(4):
                    gemm_tile(pe, (i, 4, T_MO + k), OC)
            norm_pe(pe, "ffn", H)
            pe.wait_ge(norm_ready, 4)

            pe.wait_ge(pk["keys_in"], 16)
            with pe.Fori(0, 4) as i:
                for k in range(4):
                    gemm_tile(pe, (i, 4, T_PQ + k), H)
                    pe.wait_ge(pk["qs"], i * 4 + k + 1)
                    key = skT[:, bass.ds(i * 4 + k, 1), :].rearrange("p o n -> p (o n)")
                    b = 4 + 2 * (k % 2)
                    pe.wait_ge(pk["sev"], i * 4 + (k + 1))
                    for q in range(QT):
                        rows = P if q < 4 else NS
                        out = psum[0:rows, b + q // 4, (q % 4) * P:(q % 4 + 1) * P]
                        mm = nc.tensor.matmul(out, qps[:, k, q * P:q * P + rows], key, start=True, stop=True)
                    mm.then_inc(pk["s"], 1)
            with pe.Fori(0, QT) as q:
                pe.wait_ge(pk["sl"], q + 1)
                for j in range(3):
                    mm = nc.tensor.transpose(psum[:, 4, j * P:(j + 1) * P], slots[:, j, :], ident)
                mm.then_inc(pk["slT"], 1)
            with pe.Fori(0, NT // 8) as i:
                for b in range(2):
                    pe.wait_ge(pk["oh"], i * 2 + (b + 1))
                    for n in range(4):
                        mm = nc.tensor.matmul(psum[:, 6 + b, n * P:(n + 1) * P], OH2[b][:, n, :], OH1[b][:, n, :],
                                              start=True, stop=True)
                    mm.then_inc(pk["g"], 1)

            def expert_u(group, reg=None):
                for k in range(R):
                    tile = T_U + group * R + k
                    gemm_tile(pe, tile if reg is None else (reg, 2 * R, tile), H)

            def expert_v(group, reg=None):
                n = group + 1
                pe.wait_ge(v_full, 16 * n if reg is None else reg * 32 + 16 * n)
                pe.wait_ge(coef_ready, 4 * n if reg is None else reg * 8 + 4 * n)
                for d in range(KD):
                    y = group * KD + d
                    pe.wait_ge(y_free, y + 1 if reg is None else reg * (2 * KD) + (y + 1))
                    for k in range(R):
                        for b in range(2):
                            mm = nc.tensor.matmul(aux[d % 2][:, b, :], vring[:, k, d * P:(d + 1) * P],
                                                  coef[group % 2][:, k, b * HN:(b + 1) * HN],
                                                  start=(k == 0), stop=(k == R - 1))
                    mm.then_inc(y_full, 1)
                pe.drain().then_inc(v_done, 1)

            pe.sem_inc(v_done, 2)
            pe.wait_ge(pk["gev"], NT // 4 + 2)
            expert_u(0)
            with pe.Fori(0, NG // 2 - 1) as i:
                expert_u(1, i)
                expert_v(0, i)
                expert_u(2, i)
                expert_v(1, i)
            expert_u(NG - 1)
            expert_v(NG - 2)
            expert_v(NG - 1)
            norm_pe(pe, "final", H)

        @block.scalar
        def _(act):
            act.wait_ge(consts_in, 32)
            act.wait_ge(mem_in, 16)
            norm_act(act, "mem", memT, hmT)
            for g in range(4):
                act.wait_ge(tile_done, T_MV + 4 * g + 4)
                if g >= 2:
                    act.wait_ge(stage_out[g % 2], 16)
                nc.scalar.activation(stage[g % 2], psum[:, 2 * (g % 2):2 * (g % 2) + 2, :], ACT.Copy)\
                    .then_inc(mv_free, 1)
                act.drain().then_inc(staged, 1)
            for n in range(KD):
                act.wait_ge(tile_done, T_MK + n + 1)
                act.wait_ge(stage_out[n % 2], 16 * (2 + n // 2))
                nc.scalar.activation(stage[n % 2][:, 0, 0:MEM], psum[:, 2 * (n % 2), 0:MEM], ACT.Copy)\
                    .then_inc(acc_free, 1)
                act.drain().then_inc(staged, 1)
            act.wait_ge(x_in, 16)
            norm_act(act, "mix", X, H)
            act.wait_ge(lam_parts, 1)
            nc.scalar.activation(lamb[:, 2:4], lamb[:, 0:2], ACT.Exp).then_inc(lam_exp, 1)
            act.wait_ge(ba_full, 1)
            act.wait_ge(zeroed, 2)
            ba = psum[:, 6:8, 0:HN]

            def halves(ap):
                return ap.rearrange("p (h n) -> p h n", n=HN)
            bgw = BG[:, 0:NT]
            dt, al = sml("dt_bias")[32:40, :], sml("a_log")[32:40, :]
            nc.scalar.activation(halves(bgw[0:8, :]), ba[0:8], ACT.Sigmoid)
            nc.scalar.activation(halves(bgt[32:40, 0:NT]), ba[32:40], ACT.Abs, bias=dt)
            nc.scalar.activation(halves(bgw[32:40, :]), ba[32:40], ACT.Relu, bias=dt).then_inc(ba_free, 1)
            act.drain()
            nc.scalar.activation(bgt[32:40, 0:NT], bgt[32:40, 0:NT], ACT.Exp, scale=-1.0)
            nc.scalar.activation(lamb[32:40, 6:7], al, ACT.Exp)
            act.drain()
            nc.scalar.activation(bgt[32:40, 0:NT], bgt[32:40, 0:NT], ACT.Ln, bias=1.0).then_inc(ba_parts, 1)

            state = sml("conv_state").rearrange("p (c n) -> p c n", n=3)
            act.wait_ge(zeroed, 1)
            with act.Fori(0, HEADS) as i:
                for j in range(3):
                    tail = state[:, bass.ds(i * 3 + j, 1), :].rearrange("p o n -> p (o n)")
                    act.wait_ge(tile_done, done(T_GDN + j, i, 4))
                    a = acc[(T_GDN + j) % 2]
                    nc.scalar.activation(xp[:, j, 3 + NP_:6 + NP_], tail, ACT.Copy)
                    nc.scalar.activation(xp[:, j, 3:3 + HN], a[:, 0, :], ACT.Copy)
                    nc.scalar.activation(xp[:, j, 3 + HN:3 + NP_], a[:, 1, 0:NP_ - HN], ACT.Copy)
                    nc.scalar.activation(xp[:, j, 6 + NP_:6 + NT], a[:, 1, NP_ - HN:HN], ACT.Copy)\
                        .then_inc(acc_free, 1)
                    act.drain().then_inc(raw_ready, 1)
                    act.wait_ge(conv_done, i * 3 + (j + 1))
                    if j < 2:
                        nc.scalar.activation(cq[:, j, 0:NP_], yc[:, j, 0:NP_], ACT.Silu)
                        nc.scalar.activation(cq[:, j, NP_:NT], yc[:, j, NP_ + 3:], ACT.Silu)
                        act.drain()
                        nc.scalar.activation(sqk[:, j, :], cq[:, j, :], ACT.Square).then_inc(qk_sq, 1)
                    else:
                        v = QKV[:, bass.ds(i + 2 * HEADS, 1), :].rearrange("p o n -> p (o n)")
                        nc.scalar.activation(v[:, 0:NP_], yc[:, j, 0:NP_], ACT.Silu)
                        nc.scalar.activation(v[:, NP_:NT], yc[:, j, NP_ + 3:], ACT.Silu)
                z = OA[:, bass.ds(i, 1), 0:NT].rearrange("p o (h n) -> p (o h) n", n=HN)
                act.wait_ge(tile_done, done(T_GDN + 3, i, 4))
                nc.scalar.activation(z, acc[1], ACT.Silu).then_inc(acc_free, 1)
                act.wait_ge(qk_ss, i + 1)
                for j in range(2):
                    sq = nc.scalar.activation(halves(rqk[:, j, 0:NT]), aux[j], ACT.Sqrt, bias=eps)
                sq.then_inc(qk_root, 1)

            def gdn_block(c, dyn):
                one = c + 1
                nc.scalar.activation(Qc, QKV[:, 0:HEADS, dyn], ACT.Copy)
                nc.scalar.activation(bc, BG[:, dyn], ACT.Copy).then_inc(s["c_qb"], 1)
                act.wait_ge(s["p_kt"], one)
                nc.scalar.activation(Kt[0:CH], two(4, CH), ACT.Copy).then_inc(s["a_kvt"], 1)
                act.wait_ge(s["p_vt"], one)
                nc.scalar.activation(Vt[0:CH], two(6, CH), ACT.Copy).then_inc(s["a_kvt"], 1)
                act.wait_ge(s["d_dd"], one)
                nc.scalar.activation(ET[0:CH], ET[0:CH], ACT.Exp)
                nc.scalar.activation(ES[0:CH], ES[0:CH], ACT.Exp)
                nc.scalar.activation(ek.unsqueeze(2), Dd[0:CH, :, CH - 1:CH], ACT.Exp)
                nc.scalar.activation(EG, hc(b8[1]), ACT.Exp).then_inc(s["a_exp"], 1)
                for lv in range(1, LEVELS):
                    act.wait_ge(s["p_x"], c * LEVELS + (lv + 1))
                    nc.scalar.activation(XS[0:CH], hc(b8[0])[0:CH], ACT.Copy).then_inc(s["a_x"], 1)
                act.wait_ge(s["p_vn"], one)
                nc.scalar.activation(VN[0:CH], two(6, CH), ACT.Copy).then_inc(s["a_vn"], 1)
                act.wait_ge(s["p_o"], one)
                nc.scalar.activation(sqo, hc(b8[3]), ACT.Square).then_inc(s["a_o"], 1)
                nc.scalar.activation(oS, hc(b8[3]), ACT.Copy)
                act.wait_ge(s["p_oss"], one)
                nc.scalar.activation(rto, hc(b8[1]), ACT.Sqrt, bias=eps, scale=1.0 / DH).then_inc(s["a_rto"], 1)

            act.wait_ge(ba_done, 1)
            act.wait_ge(qk_done, HEADS)
            with act.Fori(0, NCH) as c:
                gdn_block(c, bass.ds(c * CH, CH))
            gdn_block(NCH, slice(NP_, NPAD))

            act.wait_ge(s["d_o"], NCH + 1)
            act.wait_ge(outs, 48)
            with act.Fori(0, HEADS) as h:
                for j, (dst, scale) in enumerate(((qh, 0.125), (kh, 1.0), (vh, 1.0))):
                    act.wait_ge(tile_done, done(T_DIFF + j, h, 4))
                    nc.scalar.activation(halves(dst), acc[j % 2], ACT.Copy, scale=scale).then_inc(acc_free, 1)
                    act.drain().then_inc(at["qkv"], 1)
                act.wait_ge(tile_done, done(T_DIFF + 3, h, 4))
                gate = M[:, bass.ds(h, 1), :].rearrange("p o (h n) -> p (o h) n", n=HN)
                nc.scalar.activation(gate, acc[1], ACT.Sigmoid).then_inc(acc_free, 1)
                act.wait_ge(at["pvt"], h + 1)
                nc.scalar.activation(vt[:, 0:4, :], psum[:, 6, :].rearrange("p (b n) -> p b n", b=4), ACT.Copy)
                nc.scalar.activation(vt[0:NS, 4, :], psum[0:NS, 7, 0:P], ACT.Copy).then_inc(at["vt"], 1)
                for q in range(QT):
                    w = P * (q + 1) if q < 4 else NT
                    rows = P if q < 4 else NS
                    for m in range(2):
                        act.wait_ge(at["m"], h * 10 + (2 * q + m + 1))
                        nc.scalar.activation(sc[0:rows, m, 0:w], sc[0:rows, m, 0:w], ACT.Exp,
                                             bias=mx[0:rows, m:m + 1], accum_out=zz[0:rows, m:m + 1])\
                            .then_inc(at["e"], 1)
                    act.wait_ge(at["pT"], h * 5 + q + 1)
                    if q < 4:
                        nc.scalar.activation(aT[:, 0:q + 1, :],
                                             psum[:, 6, 0:w].rearrange("p (b n) -> p b n", n=P),
                                             ACT.Copy).then_inc(at["aT"], 1)
                    else:
                        nc.scalar.activation(aT[0:NS, 1, 0:NS], psum[0:NS, 6, P:P + NS], ACT.Copy)
                        nc.scalar.activation(aT[:, 0, :], psum[:, 6, 0:P], ACT.Copy).then_inc(at["aT"], 1)
                    if q == 3:
                        act.wait_ge(at["o"], h * 5 + 4)
                        nc.scalar.activation(ob[:, 0:NP_], psum[:, 7, :], ACT.Copy)
                        act.drain()
                        nc.scalar.activation(osq[:, 0:NP_], ob[:, 0:NP_], ACT.Square).then_inc(at["obs"], 1)
                act.wait_ge(at["o"], h * 5 + 5)
                nc.scalar.activation(ob[:, NP_:NT], psum[:, 7, 0:NS], ACT.Copy)
                act.drain()
                nc.scalar.activation(osq[:, NP_:NT], ob[:, NP_:NT], ACT.Square).then_inc(at["obs"], 1)
                act.wait_ge(at["oss"], h + 1)
                nc.scalar.activation(ort, aux[0], ACT.Sqrt, bias=eps, scale=1.0 / DH).then_inc(at["rt"], 1)
                act.wait_ge(at["rows_out"], h * 32 + 32)

            with act.Fori(0, 2) as i:
                for k in range(4):
                    gate = M[:, bass.ds(i * 4 + (HEADS + k), 1), :].rearrange("p o (h n) -> p (o h) n", n=HN)
                    act.wait_ge(tile_done, done(T_GATE + k, i, 4))
                    nc.scalar.activation(gate, acc[k % 2], ACT.Sigmoid).then_inc(acc_free, 1)
            act.drain()
            with act.Fori(0, 8) as i:
                for d in range(2):
                    act.wait_ge(tile_done, done(T_MERGE + 2 * d, i, 4))
                    act.wait_ge(merged, i * 2 + (d + 1))
                    nc.scalar.activation(sgb, acc[0], ACT.Sigmoid).then_inc(acc_free, 1)
                    act.drain().then_inc(gates_ready, 1)

            act.wait_ge(x_done, 1)
            norm_act(act, "cross", X, H)
            act.wait_ge(norm_ready, 3)
            with act.Fori(0, 4) as i:
                for k in range(4):
                    dst = M[:, bass.ds(i * 4 + k, 1), :].rearrange("p o (h n) -> p (o h) n", n=HN)
                    act.wait_ge(tile_done, done(T_MQ + k, i, 4))
                    nc.scalar.activation(dst, acc[k % 2], ACT.Copy, scale=MD ** -0.5).then_inc(acc_free, 1)
            act.drain()
            act.sem_inc(ca["oev"], 2)
            with act.Fori(0, MH) as h:
                nc.scalar.activation(qst, M[:, bass.ds(h * 4, 4), :], ACT.Copy).then_inc(ca["T"], 1)
                act.wait_ge(ca["m"], h * 2 + 1)
                for q in range(4):
                    ex = nc.scalar.activation(pm[:, q, :], psum[:, 4 + q // 2, (q % 2) * MEM:(q % 2 + 1) * MEM],
                                              ACT.Exp, bias=mst[:, q:q + 1], accum_out=mst[:, 5 + q:6 + q])
                ex.then_inc(ca["e"], 1)
                act.wait_ge(ca["m"], h * 2 + 2)
                nc.scalar.activation(pms[0:NS, :], psum[0:NS, 6, 0:MEM], ACT.Exp, bias=mst[0:NS, 4:5],
                                     accum_out=mst[0:NS, 9:10]).then_inc(ca["e"], 1)
                act.wait_ge(ca["pT"], h * 2 + 1)
                nc.scalar.activation(pmT, psum[:, 4:6, :], ACT.Copy).then_inc(ca["T"], 1)
                act.wait_ge(ca["pT"], h * 2 + 2)
                nc.scalar.activation(pmTs, psum[:, 6, 0:2 * NS].rearrange("p (b n) -> p b n", b=2),
                                     ACT.Copy).then_inc(ca["T"], 1)
                for k in range(4):
                    o = OC[:, bass.ds(h * 4 + k, 1), :].rearrange("p o n -> p (o n)")
                    act.wait_ge(ca["o"], h * 4 + (k + 1))
                    nc.scalar.activation(o[:, 0:NP_], psum[:, 2 * (k % 2), :], ACT.Copy)
                    nc.scalar.activation(o[:, NP_:NT], psum[:, 2 * (k % 2) + 1, 0:NS], ACT.Copy)\
                        .then_inc(ca["oev"], 1)
            act.wait_ge(x_done, 2)
            norm_act(act, "ffn", X, H)
            act.wait_ge(norm_ready, 4)
            with act.Fori(0, 4) as i:
                for k in range(4):
                    act.wait_ge(tile_done, done(T_PQ + k, i, 4))
                    nc.scalar.activation(halves(qps[:, k, :]), acc[k % 2], ACT.Copy).then_inc(acc_free, 1)
                    act.drain().then_inc(pk["qs"], 1)
            with act.Fori(0, QT) as q:
                cols = slotT[:, :, bass.ds(q * P, P)]
                act.wait_ge(pk["top"], q + 1)
                nc.scalar.activation(bestv, bestv, ACT.Exp).then_inc(pk["gexp"], 1)
                act.wait_ge(pk["slT"], q + 1)
                nc.scalar.activation(cols, psum[:, 4, 0:3 * P].rearrange("p (j n) -> p j n", j=3), ACT.Copy)\
                    .then_inc(pk["slTe"], 1)
            act.sem_inc(pk["gev"], 2)
            for g in range(NT // GT):
                if g:
                    act.wait_ge(pk["stored"], 32 * g)
                with act.Fori(0, GT // 8) as i:
                    for b in range(2):
                        dst = Gs[:, :, bass.ds(i * 8 + 4 * b, 4)].rearrange("p a n -> p n a")
                        act.wait_ge(pk["g"], i * 2 + (g * (GT // 4) + b + 1))
                        nc.scalar.activation(dst, psum[:, 6 + b, :].rearrange("p (n a) -> p n a", n=4),
                                             ACT.Copy).then_inc(pk["gev"], 1)
            with act.Fori(0, NG) as g:
                for k in range(R):
                    b = k % 2
                    act.wait_ge(tile_done, done(T_U + k, g, R))
                    act.wait_ge(hid_free, g * R + (k + 1))
                    nc.scalar.activation(halves(hid[:, b, :]), acc[b], ACT.Gelu_apprx_tanh).then_inc(acc_free, 1)
                    act.drain().then_inc(hid_ready, 1)
            act.wait_ge(x_done, 3)
            norm_act(act, "final", X, H)

        @block.vector
        def _(dve):
            dve.wait_ge(consts_in, 32)
            lm = sml("lambdas").rearrange("p (a n) -> p a n", a=4)
            for a in range(2):
                nc.vector.tensor_tensor(tmp[:, 6000 + 64 * a:6064 + 64 * a], lm[:, 2 * a, :], lm[:, 2 * a + 1, :],
                                        ALU.mult)
            dve.drain()
            nc.vector.tensor_reduce(lamb[:, 0:2], tmp[:, 6000:6128].rearrange("p (a n) -> p a n", a=2), AX.X,
                                    ALU.add).then_inc(lam_parts, 1)
            nc.vector.tensor_scalar(g_diff8, sml("g_diff"), 1.0 - LAM_INIT, None, ALU.mult)
            norm_dve(dve, "mem", memT, hmT, sml("g_mem"))
            norm_dve(dve, "mix", X, H, sml("g_mix"))
            dve.wait_ge(lam_exp, 1)
            nc.vector.tensor_tensor(lamb[:, 3:4], lamb[:, 2:3], lamb[:, 3:4], ALU.subtract)
            dve.drain()
            nc.vector.tensor_scalar(nlam, lamb[:, 3:4], -1.0, -LAM_INIT, ALU.mult, ALU.add)
            dve.wait_ge(ba_parts, 1)
            gr = BG[32:40, 0:NT]
            nc.vector.tensor_tensor(gr, gr, bgt[32:40, 0:NT], ALU.add)
            dve.drain()
            nc.vector.tensor_scalar(gr, gr, lamb[32:40, 6:7], -1.0, ALU.mult, ALU.mult).then_inc(ba_done, 1)
            cw = sml("conv_w")
            for b in range(2):
                dve.wait_ge(stage_out[b], 16 * 10)
            with dve.Fori(0, HEADS) as i:
                for j in range(3):
                    n = NP_ + 3 + NS
                    dve.wait_ge(raw_ready, i * 3 + (j + 1))
                    nc.vector.tensor_scalar(yc[:, j, :], xp[:, j, 0:n], cw[:, bass.ds(i * 12 + 4 * j, 1)], None,
                                            ALU.mult)
                    for tap in range(1, 4):
                        dve.drain()
                        nc.vector.scalar_tensor_tensor(
                            out=yc[:, j, :], in0=xp[:, j, tap:tap + n],
                            scalar=cw[:, bass.ds(i * 12 + (4 * j + tap), 1)], in1=yc[:, j, :],
                            op0=ALU.mult, op1=ALU.add)
                    cs = conv_out[:, bass.ds(i, 1), 6 * j:6 * j + 6].rearrange("p o n -> p (o n)")
                    nc.vector.tensor_copy(cs[:, 0:3], xp[:, j, NP_:NP_ + 3])
                    nc.vector.tensor_copy(cs[:, 3:6], xp[:, j, NT + 3:NT + 6])
                    dve.drain().then_inc(conv_done, 1)
                dve.wait_ge(qk_root, i + 1)
                nc.vector.reciprocal(rqk[:, 0:2, 0:NT], rqk[:, 0:2, 0:NT])
                dve.drain()
                for j in range(2):
                    dst = QKV[:, bass.ds(i + j * HEADS, 1), 0:NT].rearrange("p o n -> p (o n)")
                    nc.vector.scalar_tensor_tensor(out=dst, in0=cq[:, j, :], scalar=DH ** -0.5 if j == 0 else 1.0,
                                                   in1=rqk[:, j, 0:NT], op0=ALU.mult, op1=ALU.mult)
                dve.drain().then_inc(qk_done, 1)

            beta3 = bg[:, 0:HEADS].unsqueeze(2)

            def over_heads(mask):
                return mask.unsqueeze(1).to_broadcast([CH, HEADS, CH])

            def gdn_block(c, dyn, S):
                one = c + 1
                nc.vector.tensor_copy(Kc, QKV[:, HEADS:2 * HEADS, dyn])
                nc.vector.tensor_copy(Vc, QKV[:, 2 * HEADS:3 * HEADS, dyn]).then_inc(s["c_kv"], 1)
                dve.wait_ge(s["p_bg"], one)
                nc.vector.tensor_copy(bg, b8[0][0:CH, 0:CH])
                dve.drain()
                nc.vector.tensor_tensor(gU[0:CH], bg[:, 32:40].unsqueeze(2).to_broadcast([CH, HEADS, CH]),
                                        over_heads(cst("upper", CH)), ALU.mult).then_inc(s["d_gu"], 1)
                dve.wait_ge(s["p_g"], one)
                nc.vector.tensor_copy(gcol, b8[0][0:CH, 64:72])
                dve.drain()
                nc.vector.tensor_tensor(Dd[0:CH], hc(b8[1])[0:CH],
                                        gcol.unsqueeze(2).to_broadcast([CH, HEADS, CH]), ALU.subtract)
                dve.drain()
                nc.vector.tensor_tensor(ET[0:CH], Dd[0:CH], over_heads(cst("ge", CH)), ALU.mult)
                nc.vector.tensor_tensor(ES[0:CH], Dd[0:CH], over_heads(cst("nstrict", CH)), ALU.mult)
                dve.drain().then_inc(s["d_dd"], 1)
                dve.wait_ge(s["a_exp"], one)
                dve.wait_ge(s["p_kk"], one)
                nc.vector.tensor_tensor(ES[0:CH], ES[0:CH], over_heads(cst("strict", CH)), ALU.mult)
                nc.vector.tensor_tensor(ET[0:CH], ET[0:CH], over_heads(cst("ge", CH)), ALU.mult)
                dve.drain()
                nc.vector.tensor_tensor(A[0:CH], hc(b8[2])[0:CH], ES[0:CH], ALU.mult)
                dve.drain()
                nc.vector.tensor_tensor(A[0:CH], A[0:CH], beta3.to_broadcast([CH, HEADS, CH]), ALU.mult)
                dve.drain()
                nc.vector.tensor_tensor(Bl[0:CH], A[0:CH], over_heads(levels[:, 0, :]), ALU.mult)\
                    .then_inc(s["d_a"], 1)
                nc.vector.tensor_tensor(QKT[0:CH], hc(b8[3])[0:CH], ET[0:CH], ALU.mult)
                dve.wait_ge(s["a_kvt"], c * 2 + 2)
                nc.vector.tensor_tensor(kd[0:CH], Kt[0:CH], ek.unsqueeze(2).to_broadcast([CH, HEADS, DH]), ALU.mult)
                nc.vector.tensor_tensor(kg, Kc, EG, ALU.mult)
                nc.vector.tensor_tensor(qd, Qc, EG, ALU.mult)
                idh = over_heads(ident[0:CH, 0:CH])
                dve.wait_ge(s["p_x"], c * LEVELS + 1)
                nc.vector.tensor_tensor(Rt[0:CH], idh, hc(b8[0])[0:CH], ALU.subtract)
                nc.vector.tensor_tensor(Tt[0:CH], idh, Bl[0:CH], ALU.subtract)
                dve.drain()
                nc.vector.tensor_tensor(Bl[0:CH], A[0:CH], over_heads(levels[:, 1, :]), ALU.mult)\
                    .then_inc(s["d_r"], 1)
                for lv in range(1, LEVELS):
                    dve.wait_ge(s["p_rt"], c * (LEVELS - 1) + lv)
                    nc.vector.tensor_tensor(Rt[0:CH], Rt[0:CH], hc(b8[1])[0:CH], ALU.subtract)
                    nc.vector.tensor_tensor(Tt[0:CH], Tt[0:CH], hc(b8[2])[0:CH], ALU.subtract)
                    if lv + 1 < LEVELS:
                        nc.vector.tensor_tensor(Bl[0:CH], A[0:CH], over_heads(levels[:, lv + 1, :]), ALU.mult)
                    dve.drain().then_inc(s["d_r"], 1)
                dve.wait_ge(s["p_ks"], one)
                nc.vector.tensor_tensor(Vt[0:CH], Vt[0:CH], two(4, CH), ALU.subtract)
                dve.drain()
                nc.vector.tensor_tensor(Vt[0:CH], Vt[0:CH], beta3.to_broadcast([CH, HEADS, DH]), ALU.mult)\
                    .then_inc(s["d_rr"], 1)
                dve.wait_ge(s["p_s"], one)
                nc.vector.tensor_tensor(S, S, EG[:, :, CH - 1:CH].to_broadcast([P, HEADS, DH]), ALU.mult)
                dve.drain()
                nc.vector.tensor_tensor(S, S, two(4), ALU.add)
                dve.drain().then_inc(s["d_s"], 1)
                dve.wait_ge(s["a_rto"], one)
                nc.vector.reciprocal(rto, rto)
                dve.drain()
                nc.vector.tensor_tensor(oS, oS, rto, ALU.mult)
                dve.drain()
                nc.vector.scalar_tensor_tensor(out=OA[:, :, dyn], in0=oS, scalar=sml("g_gdn"), in1=OA[:, :, dyn],
                                               op0=ALU.mult, op1=ALU.mult)
                dve.drain().then_inc(s["d_o"], 1)

            dve.wait_ge(zeroed, 3)
            with dve.Fori(0, NCH) as c:
                gdn_block(c, bass.ds(c * CH, CH), Sp)
            dve.wait_ge(state_in, 16)
            gdn_block(NCH, slice(NP_, NPAD), Ss)

            dve.wait_ge(at["dist_in"], 32)
            slopes = cst("slopes")
            with dve.Fori(0, HEADS) as h:
                slope = slopes[:, bass.ds(h, 1)]
                for q in range(QT):
                    w = P * (q + 1) if q < 4 else NT
                    rows = P if q < 4 else NS
                    for m in range(2):
                        dve.wait_ge(at["s"], h * 10 + (2 * q + m + 1))
                        if q < 4:
                            nc.vector.scalar_tensor_tensor(
                                out=sc[:, m, 0:w], in0=ndist[:, q, 0:w], scalar=slope, in1=psum[:, 4 + m, 0:w],
                                op0=ALU.mult, op1=ALU.add)
                        else:
                            nc.vector.scalar_tensor_tensor(
                                out=sc[0:NS, m, 0:NP_], in0=ndist_s[0:NS, 0:NP_], scalar=slope[0:NS],
                                in1=psum[0:NS, 4 + m, :], op0=ALU.mult, op1=ALU.add)
                            nc.vector.scalar_tensor_tensor(
                                out=sc[0:NS, m, NP_:NT], in0=ndist_s[0:NS, NP_:NT], scalar=slope[0:NS],
                                in1=psum[0:NS, 7 - m, 64 * m:64 * m + NS], op0=ALU.mult, op1=ALU.add)
                        dve.drain()
                        nc.vector.tensor_reduce(mx[0:rows, m:m + 1], sc[0:rows, m, 0:w], AX.X, ALU.max, negate=True)\
                            .then_inc(at["m"], 1)
                    dve.wait_ge(at["e"], h * 10 + (2 * q + 2))
                    nc.vector.reciprocal(rz[0:rows, :], zz[0:rows, :])
                    dve.drain()
                    nc.vector.tensor_tensor(rz[0:rows, 1:2], rz[0:rows, 1:2], nlam[0:rows], ALU.mult)
                    nc.vector.tensor_scalar(sc[0:rows, 0, 0:w], sc[0:rows, 0, 0:w], rz[0:rows, 0:1], None, ALU.mult)
                    dve.drain()
                    nc.vector.scalar_tensor_tensor(out=pr[0:rows, 0:w], in0=sc[0:rows, 1, 0:w],
                                                   scalar=rz[0:rows, 1:2], in1=sc[0:rows, 0, 0:w],
                                                   op0=ALU.mult, op1=ALU.add).then_inc(at["a"], 1)
                dst = OB[:, bass.ds(h, 1), :].rearrange("p o (h n) -> p (o h) n", n=HN)
                dve.wait_ge(at["rt"], h + 1)
                nc.vector.reciprocal(ort, ort)
                dve.drain()
                nc.vector.scalar_tensor_tensor(out=dst, in0=ob.rearrange("p (h n) -> p h n", n=HN), scalar=g_diff8,
                                               in1=ort, op0=ALU.mult, op1=ALU.mult).then_inc(at["done"], 1)

            dve.sem_inc(merged, 1)
            with dve.Fori(0, 8) as i:
                for d in range(2):
                    tile = T_MERGE + 2 * d + 1
                    dst = M[:, bass.ds(i * 2 + d, 1), :].rearrange("p o (h n) -> p (o h) n", n=HN)
                    dve.wait_ge(gates_ready, i * 2 + (d + 1))
                    dve.wait_ge(tile_done, done(tile, i, 4))
                    nc.vector.tensor_tensor(t1, dst, acc[1], ALU.mult)
                    nc.vector.tensor_tensor(sgb, sgb, aux[d % 2], ALU.mult).then_inc(acc_free, 1)
                    dve.drain()
                    nc.vector.tensor_tensor(dst, t1, sgb, ALU.add)
                    dve.drain().then_inc(merged, 1)

            def residual(first):
                with dve.Fori(0, 4) as i:
                    for k in range(4):
                        dst = X[:, bass.ds(i * 4 + k, 1), :].rearrange("p o (h n) -> p (o h) n", n=HN)
                        dve.wait_ge(tile_done, done(first + k, i, 4))
                        nc.vector.tensor_tensor(dst, dst, acc[k % 2], ALU.add).then_inc(acc_free, 1)
                dve.drain().then_inc(x_done, 1)

            dve.wait_ge(x_again, 16)
            residual(T_OUT)
            norm_dve(dve, "cross", X, H, sml("g_cross"))

            with dve.Fori(0, MH) as h:
                dve.wait_ge(ca["s"], h * 2 + 1)
                nc.vector.tensor_reduce(mst[:, 0:4], psum[:, 4:6, :].rearrange("p b (q n) -> p (b q) n", n=MEM),
                                        AX.X, ALU.max, negate=True).then_inc(ca["m"], 1)
                dve.wait_ge(ca["s"], h * 2 + 2)
                nc.vector.tensor_reduce(mst[0:NS, 4:5], psum[0:NS, 6, 0:MEM], AX.X, ALU.max, negate=True)\
                    .then_inc(ca["m"], 1)
                dve.wait_ge(ca["e"], h * 2 + 1)
                nc.vector.reciprocal(mst[:, 10:14], mst[:, 5:9])
                dve.drain()
                nc.vector.tensor_tensor(pm, pm, mst[:, 10:14].unsqueeze(2).to_broadcast([P, 4, MEM]), ALU.mult)\
                    .then_inc(ca["p"], 1)
                dve.wait_ge(ca["e"], h * 2 + 2)
                nc.vector.reciprocal(mst[0:NS, 14:15], mst[0:NS, 9:10])
                dve.drain()
                nc.vector.tensor_scalar(pms[0:NS, :], pms[0:NS, :], mst[0:NS, 14:15], None, ALU.mult)\
                    .then_inc(ca["p"], 1)
            residual(T_MO)
            norm_dve(dve, "ffn", X, H, sml("g_ffn"))

            nc.vector.memset(SC[:, 4, :], 0.0)
            dve.drain()
            dve.sem_inc(pk["sev"], 1)
            with dve.Fori(0, 4) as i:
                for k in range(4):
                    b = 4 + 2 * (k % 2)
                    dst = SC[:, 0:4, bass.ds((i * 4 + k) * P, P)]
                    dst4 = SC[0:NS, 4, bass.ds((i * 4 + k) * P, P)]
                    dve.wait_ge(pk["s"], i * 4 + (k + 1))
                    nc.vector.tensor_copy(dst, psum[:, b, :].rearrange("p (q n) -> p q n", q=4))
                    nc.vector.tensor_copy(dst4, psum[0:NS, b + 1, 0:P])
                    dve.drain().then_inc(pk["sev"], 1)
            NEG = -3.0e38
            with dve.Fori(0, QT) as q:
                src = SC[:, bass.ds(q, 1), :].rearrange("p o (c n) -> p (o c) n", n=NKEY)
                nc.vector.tensor_copy(sct, src)
                dve.drain()
                for c in range(2 * HEADS):
                    nc.vector.max(tv[:, c, 0:8], sct[:, c, :])
                dve.drain()
                for c in range(2 * HEADS):
                    nc.vector.max_index(tiu[:, c, 0:8], tv[:, c, 0:8], sct[:, c, :])
                for c in range(2 * HEADS):
                    nc.vector.match_replace(work[:, c, :], tv[:, c, 0:8], sct[:, c, :], NEG)
                dve.drain()
                for c in range(2 * HEADS):
                    nc.vector.max(tv[:, c, 8:16], work[:, c, :])
                dve.drain()
                for c in range(2 * HEADS):
                    nc.vector.max_index(tiu[:, c, 8:16], tv[:, c, 8:16], work[:, c, :])
                dve.drain()
                nc.vector.tensor_copy(tif, tiu[:, :, :])
                tv4 = tv.rearrange("p (h s) n -> p h s n", s=2)
                cand = sct.rearrange("p (h s) n -> p h (s n)", s=2)
                nc.vector.tensor_tensor(cand.rearrange("p h (a b) -> p h a b", a=TOPK),
                                        tv4[:, :, 0, :].unsqueeze(3).to_broadcast([P, HEADS, TOPK, TOPK]),
                                        tv4[:, :, 1, :].unsqueeze(2).to_broadcast([P, HEADS, TOPK, TOPK]), ALU.add)
                dve.drain()
                cwork = work.rearrange("p (h s) n -> p h (s n)", s=2)
                for c in range(HEADS):
                    nc.vector.max(bestv[:, c, 0:8], cand[:, c, :])
                dve.drain()
                for c in range(HEADS):
                    nc.vector.max_index(selu[:, 0, c, 0:8], bestv[:, c, 0:8], cand[:, c, :])
                for c in range(HEADS):
                    nc.vector.match_replace(cwork[:, c, :], bestv[:, c, 0:8], cand[:, c, :], NEG)
                dve.drain()
                for c in range(HEADS):
                    nc.vector.max(bestv[:, c, 8:16], cwork[:, c, :])
                dve.drain()
                for c in range(HEADS):
                    nc.vector.max_index(selu[:, 0, c, 8:16], bestv[:, c, 8:16], cwork[:, c, :])
                nc.vector.tensor_copy(zs[:, 0, :], bestv[:, :, 0])
                dve.drain()
                nc.vector.tensor_tensor(bestv, bestv, zs[:, 0, :].unsqueeze(2).to_broadcast([P, HEADS, TOPK]),
                                        ALU.subtract)
                dve.drain().then_inc(pk["top"], 1)
                nc.vector.tensor_scalar(selu[:, 1], selu[:, 0], 4, None, ALU.logical_shift_right)
                nc.vector.tensor_scalar(selu[:, 2], selu[:, 0], 15, None, ALU.bitwise_and)
                dve.drain()
                nc.vector.tensor_copy(abf.rearrange("p s (h k) -> p s h k", h=HEADS), selu[:, 1:3])
                tif4 = tif.rearrange("p (h s) n -> p h s n", s=2)
                eq4 = eqb.rearrange("p (h k) j -> p h k j", h=HEADS)
                for a in range(2):
                    dve.drain()
                    nc.vector.tensor_tensor(eqb, abf[:, a, :].unsqueeze(2).to_broadcast([P, P, TOPK]),
                                            iota[:, 0:TOPK].unsqueeze(1).to_broadcast([P, P, TOPK]), ALU.is_equal)
                    dve.drain()
                    nc.vector.tensor_tensor(eq4, eq4, tif4[:, :, a, :].unsqueeze(2)
                                            .to_broadcast([P, HEADS, TOPK, TOPK]), ALU.mult)
                    dve.drain()
                    nc.vector.tensor_reduce(slots[:, a, :], eqb, AX.X, ALU.add)
                dve.wait_ge(pk["gexp"], q + 1)
                nc.vector.tensor_reduce(zs[:, 0, :], bestv, AX.X, ALU.add)
                dve.drain()
                nc.vector.reciprocal(zs[:, 0, :], zs[:, 0, :])
                dve.drain()
                nc.vector.tensor_tensor(slots[:, 2, :].rearrange("p (h k) -> p h k", h=HEADS), bestv,
                                        zs[:, 0, :].unsqueeze(2).to_broadcast([P, HEADS, TOPK]), ALU.mult)
                dve.drain().then_inc(pk["sl"], 1)
                dve.wait_ge(pk["slTe"], q + 1)
            with dve.Fori(0, NT // 8) as i:
                for b in range(2):
                    def col(j):
                        return slotT[:, j, bass.ds(i * 8 + 4 * b, 4)].unsqueeze(2).to_broadcast([P, 4, P])
                    row = iota.unsqueeze(1).to_broadcast([P, 4, P])
                    c1, c2, c3 = col(0), col(1), col(2)
                    dve.wait_ge(pk["gev"], i * 2 + (b + 1))
                    nc.vector.tensor_tensor(OH2[b], c2, row, ALU.is_equal)
                    nc.vector.tensor_tensor(OH1[b], c1, row, ALU.is_equal)
                    dve.drain()
                    nc.vector.tensor_tensor(OH1[b], OH1[b], c3, ALU.mult)
                    dve.drain().then_inc(pk["oh"], 1)

            dve.sem_inc(hid_free, 2)
            dve.sem_inc(y_free, 2)

            def expert_coef(group, reg=None):
                b = group % 2
                dve.wait_ge(v_done, group + 1 if reg is None else reg * 2 + (group + 1))
                n = 16 * (group // 2 + 1)
                dve.wait_ge(g_full[b], n if reg is None else reg * 16 + n)
                for k in range(R):
                    n = group * R + k + 1
                    dve.wait_ge(hid_ready, n if reg is None else reg * (2 * R) + n)
                    nc.vector.tensor_tensor(coef[b][:, k, :], hid[:, k % 2, :], gat[b][:, k, :], ALU.mult)\
                        .then_inc(hid_free, 1)
                    dve.drain().then_inc(coef_ready, 1)

            def expert_sum(group, reg=None):
                for d in range(KD):
                    n = group * KD + d + 1
                    dve.wait_ge(y_full, n if reg is None else reg * (2 * KD) + n)
                    dst = X[:, d, :].rearrange("p (h n) -> p h n", n=HN)
                    nc.vector.tensor_tensor(dst, dst, aux[d % 2], ALU.add).then_inc(y_free, 1)

            expert_coef(0)
            with dve.Fori(0, NG // 2 - 1) as i:
                expert_coef(1, i)
                expert_sum(0, i)
                expert_coef(2, i)
                expert_sum(1, i)
            expert_coef(NG - 1)
            expert_sum(NG - 2)
            dve.drain()
            expert_sum(NG - 1)
            dve.drain().then_inc(x_done, 1)
            norm_dve(dve, "final", X, H, sml("g_final"))


INPUTS = [("consts", (P, N_CONST)), ("small", (P, N_SMALL)), ("xT", (P, KD, NT)), ("memT", (P, KD, MEM)),
          ("w_ba", (P, KD, 64)), ("weights", (N_STREAM, P, D)), ("uT", (NKEY, P, D)), ("v", (NKEY, P, D)),
          ("sub_keys", (P, 2 * HEADS, NKEY)), ("state_in", (P, HEADS, DH)), ("ndist", (P, 4, NP_)),
          ("ndist_s", (NS, NT)), ("cache_k", (HEADS, P, NP_)), ("cache_v", (HEADS, P, 4, DH)),
          ("cmem_k", (KD, P, MEM)), ("cmem_v", (P, 2, D))]
OUTPUTS = [("y", (P, KD, NT)), ("k_rows", (HEADS, P, NT)), ("v_rows", (HEADS, P, NT)),
           ("mem_k", (KD, P, MEM)), ("mem_v", (P, 2, D)), ("state_p", (P, HEADS, DH)),
           ("state_s", (P, HEADS, DH)), ("conv_state", (P, HEADS, 18))]


def constants():
    c = np.zeros((P, N_CONST), np.float32)

    def put(name, a):
        o, w = CONST[name]
        a = np.asarray(a, np.float32)
        c[:a.shape[0], o:o + w] = a

    i, j = np.arange(CH)[:, None], np.arange(CH)[None, :]
    put("ident", np.eye(P))
    put("ones", np.ones((P, P)))
    put("upper", i <= j)
    put("ge", i <= j)
    put("strict", i > j)
    put("nstrict", -1.0 * (i > j))
    put("levels", np.concatenate([(i // (2 << l) == j // (2 << l)) & (i // (1 << l) % 2 == 1)
                                  & (j // (1 << l) % 2 == 0) for l in range(LEVELS)], 1))
    put("iota", np.tile(np.arange(P), (P, 1)))
    put("eps", np.full((P, 2), EPS))
    put("slopes", np.tile(2.0 ** (-8.0 * (np.arange(HEADS) + 1) / HEADS), (P, 1)))
    q, k = np.arange(NP_)[:, None], np.arange(NP_)[None, :]
    dist = np.where(k // CH <= q // CH, -np.abs(q - k), -1e30).astype(np.float32)
    qs, ks = NP_ + np.arange(NS)[:, None], np.arange(NT)[None, :]
    dist_s = np.where(ks // CH <= qs // CH, -np.abs(qs - ks), -1e30).astype(np.float32)
    return c, np.ascontiguousarray(dist.reshape(4, P, NP_).transpose(1, 0, 2)), dist_s


def tiles(w):
    K, N = w.shape
    return w.reshape(K // P, P, N // P, P).transpose(2, 1, 0, 3).reshape(N // P, P, -1)


def chunked(w):
    return w.T.reshape(w.shape[1] // P, P, w.shape[0]).transpose(1, 0, 2)


def lay_out(i):
    w_in = i["w_in"][0]
    edges = np.cumsum([0, 3072, 1024, 8, 8, 1024, 1024, 1024, D, D])
    qkv, z, b, a, dq, dk, dv, ga, gb = (w_in[:, s:e] for s, e in zip(edges[:-1], edges[1:]))
    qkv_t, z_t, dq_t, dk_t, dv_t, ga_t, gb_t = map(tiles, (qkv, z, dq, dk, dv, ga, gb))
    mv = i["w_mv"][0].reshape(4, 4, P, 4, 512).transpose(3, 0, 2, 1, 4).reshape(16, P, D)
    stream = np.empty((N_STREAM, P, D), np.float32)
    stream[T_MV:T_MV + 16] = mv
    stream[T_MK:T_MK + 16] = tiles(i["w_mk"][0])
    for j in range(3):
        stream[T_GDN + j:T_DIFF:4] = qkv_t[8 * j:8 * j + 8]
    stream[T_GDN + 3:T_DIFF:4] = z_t
    for j, w in enumerate((dq_t, dk_t, dv_t, ga_t[:8])):
        stream[T_DIFF + j:T_GATE:4] = w
    stream[T_GATE:T_MERGE] = ga_t[8:]
    stream[T_MERGE:T_OUT:2] = gb_t
    stream[T_MERGE + 1:T_OUT:2, :, :D // 2] = tiles(i["w_branch_a"][0])
    stream[T_MERGE + 1:T_OUT:2, :, D // 2:] = tiles(i["w_branch_b"][0])
    for at, name in ((T_OUT, "w_out"), (T_MQ, "w_mq"), (T_MO, "w_mo"), (T_PQ, "peer_w_q")):
        stream[at:at + 16] = tiles(i[name][0])
    w_ba = np.zeros((P, KD, 64), np.float32)
    w_ba[:, :, 0:8] = b.reshape(KD, P, 8).transpose(1, 0, 2)
    w_ba[:, :, 32:40] = a.reshape(KD, P, 8).transpose(1, 0, 2)
    small = np.zeros((P, N_SMALL), np.float32)

    def put(name, v, rows=slice(0, P)):
        o, w = SMALL[name]
        small[rows, o:o + w] = v

    for name, src in (("g_mix", "norm_mix_g"), ("g_cross", "norm_cross_g"), ("g_mem", "norm_mem_g"),
                      ("g_ffn", "norm_ffn_g")):
        put(name, i[src][0].reshape(KD, P).T)
    put("g_final", i["final_norm_g"].reshape(KD, P).T)
    put("g_gdn", i["gdn_norm_g"][0][:, None])
    put("g_diff", i["diff_subln_g"][0][:, None])
    put("dt_bias", i["gdn_dt_bias"][0][:, None], slice(32, 40))
    put("a_log", i["gdn_a_log"][0][:, None], slice(32, 40))
    put("lambdas", np.concatenate([i["diff_lambda_" + n][0] for n in ("q1", "k1", "q2", "k2")])[None, :])
    put("conv_w", i["gdn_conv_w"][0].reshape(4, 3, HEADS, P).transpose(3, 2, 1, 0).reshape(P, -1))
    put("conv_state", i["state_conv"][0, 0].reshape(3, 3, HEADS, P).transpose(3, 2, 1, 0).reshape(P, -1))
    consts, ndist, ndist_s = constants()
    x = np.concatenate([i["x_prompt"][0], i["x_sample"][0]], 0)
    cv = i["cache_diff_v"][0, 0].reshape(4, P, HEADS, DH)
    return {
        "consts": consts, "small": small, "xT": chunked(x), "memT": chunked(i["mem_prompt"][0]), "w_ba": w_ba,
        "weights": stream, "uT": tiles(i["peer_u"][0].T), "v": i["peer_v"][0].reshape(NKEY, P, D),
        "sub_keys": i["peer_sub_keys"][0].reshape(2 * HEADS, NKEY, P).transpose(2, 0, 1),
        "state_in": i["state_gdn"][0, 0].transpose(1, 0, 2), "ndist": ndist, "ndist_s": ndist_s,
        "cache_k": i["cache_diff_k"][0, 0].transpose(1, 2, 0), "cache_v": cv.transpose(2, 1, 0, 3),
        "cmem_k": i["cache_mem_k"][0, 0].reshape(MEM, KD, P).transpose(1, 2, 0),
        "cmem_v": i["cache_mem_v"][0, 0].reshape(2, P, D).transpose(1, 0, 2),
    }


def kernel(**inputs):
    import concourse.bacc as bacc
    from concourse.bass_utils import run_bass_kernel_spmd

    inputs = {k: np.asarray(v) for k, v in inputs.items()}
    nc = bacc.Bacc("TRN2", target_bir_lowering=False, num_devices=1)
    laid = lay_out(inputs)
    arrays, t = {}, {}
    for name, shape in INPUTS:
        a = np.ascontiguousarray(laid[name])
        assert a.shape == tuple(shape), (name, a.shape)
        arrays["in_" + name] = a
        t[name] = nc.dram_tensor("in_" + name, a.shape, F32, kind="ExternalInput").ap()
    for name, shape in OUTPUTS:
        t[name] = nc.dram_tensor("out_" + name, shape, F32, kind="ExternalOutput").ap()
    t["gates"] = nc.dram_tensor("gates", (P, NKEY, NT), F32, kind="Internal").ap()
    program(nc, t)
    r = run_bass_kernel_spmd(nc, [arrays], core_ids=[0]).results[0]
    o = {name: r["out_" + name] for name, _ in OUTPUTS}

    y = o["y"].transpose(2, 1, 0).reshape(NT, D)
    k_rows = o["k_rows"].transpose(2, 0, 1)
    v_rows = o["v_rows"].transpose(2, 0, 1)
    conv = o["conv_state"].reshape(P, HEADS, 3, 2, 3).transpose(3, 4, 2, 1, 0).reshape(2, 3, 3 * HEADS * P)
    mem_k = o["mem_k"].transpose(2, 0, 1).reshape(1, 1, MEM, MH, MD)
    mem_v = o["mem_v"].transpose(1, 0, 2).reshape(1, 1, MEM, MH, MD)
    return (y[None, :NP_], y[None, NP_:], k_rows[None, None, :NP_], v_rows[None, None, :NP_],
            o["state_p"].transpose(1, 0, 2)[None, None], conv[0][None, None], mem_k, mem_v,
            k_rows[None, None, NP_:], v_rows[None, None, NP_:],
            o["state_s"].transpose(1, 0, 2)[None, None], conv[1][None, None])
```

```python
from contextlib import ExitStack

import numpy as np

import concourse.bass as bass
from concourse import mybir

F32 = mybir.dt.float32
F32R = mybir.dt.float32r
U32 = mybir.dt.uint32
ACT = mybir.ActivationFunctionType
ALU = mybir.AluOpType
AX = mybir.AxisListType

P = 128
D = 2048
KD = D // P
NP_, NS = 512, 32
NT = NP_ + NS
HN = NT // 2
MEM = 256
HEADS = 8
DH = 128
CH = 64
NCH = NP_ // CH
NPAD = NP_ + CH
LEVELS = 6
MH, MD = 4, 512
EPS = 1e-6
NKEY = 128
TOPK = 16
QT = 5
R = 4
GT = 68
LAM_INIT = 0.2

T_MV, T_MK, T_GDN, T_DIFF, T_GATE = 0, 16, 32, 64, 96
T_MERGE, T_OUT, T_MQ, T_MO, T_PQ, T_U = 104, 136, 152, 168, 184, 200
N_STREAM = T_U

CONST = {}
_n = 0
for _name, _w in [("ident", P), ("ones", P), ("upper", CH), ("ge", CH), ("strict", CH), ("nstrict", CH),
                  ("levels", LEVELS * CH), ("iota", P), ("eps", 2), ("slopes", HEADS)]:
    CONST[_name] = (_n, _w)
    _n += _w
N_CONST = _n
SMALL = {}
_n = 0
for _name, _w in [("g_mix", KD), ("g_cross", KD), ("g_mem", KD), ("g_ffn", KD), ("g_final", KD),
                  ("g_gdn", 1), ("g_diff", 1), ("dt_bias", 1), ("a_log", 1), ("lambdas", 4 * 64),
                  ("conv_w", 3 * HEADS * 4), ("conv_state", 3 * HEADS * 3)]:
    SMALL[_name] = (_n, _w)
    _n += _w
N_SMALL = _n


def program(nc, t):
    with ExitStack() as ctx:
        def sem(name):
            return ctx.enter_context(nc.semaphore(name))

        base = -(-nc.sbuf_base // 32) * 32
        ring = ctx.enter_context(nc.sbuf_tensor("ring", [P, R, D], F32))
        H = ctx.enter_context(nc.sbuf_tensor("H", [P, KD, NT], F32))
        BIG = 2 * KD * NT
        OAB_N = HEADS * NPAD + HEADS * NT
        arena = ctx.enter_context(nc.sbuf_tensor("arena", [P, BIG + OAB_N], F32))
        TMP_N = 7680
        tmp = ctx.enter_context(nc.sbuf_tensor("tmp", [P, TMP_N], F32))
        const = ctx.enter_context(nc.sbuf_tensor("const", [P, N_CONST], F32))
        small = ctx.enter_context(nc.sbuf_tensor("small", [P, N_SMALL], F32))
        lamb = ctx.enter_context(nc.sbuf_tensor("lamb", [P, 8], F32))
        psum = ctx.enter_context(nc.psum_tensor("psum", [P, 8, 512], F32))

        def view(buf, start, *shape):
            n = int(np.prod(shape))
            v = buf[:, start:start + n]
            if len(shape) == 2:
                v = v.rearrange("p (a b) -> p a b", a=shape[0])
            if len(shape) == 3:
                v = v.rearrange("p (a b c) -> p a b c", a=shape[0], b=shape[1])
            return v, start + n

        def cst(name, rows=P):
            o, w = CONST[name]
            return const[0:rows, o:o + w]

        def sml(name):
            o, w = SMALL[name]
            return small[:, o:o + w]

        ident, ones, iota = cst("ident"), cst("ones"), cst("iota")
        levels = cst("levels", CH).rearrange("p (l c) -> p l c", l=LEVELS)
        eps = cst("eps")[:, 0:1]

        acc = [psum[:, 2 * b:2 * b + 2, 0:HN] for b in range(2)]
        aux = [psum[:, 4 + 2 * b:6 + 2 * b, 0:HN] for b in range(2)]

        X, _ = view(arena, 0, KD, NT)
        M, _ = view(arena, KD * NT, KD, NT)
        QKV, qkv_end = view(arena, 0, 3 * HEADS, NPAD)
        OA, _ = view(arena, BIG, HEADS, NPAD)
        OB, _ = view(arena, BIG + HEADS * NPAD, HEADS, NT)
        OC, _ = view(arena, BIG, KD, NT)
        memT, _ = view(arena, BIG, KD, MEM)
        hmT, _ = view(arena, KD * NT, KD, MEM)
        stage = [view(tmp, 2000 + 1024 * b, 2, 512)[0] for b in range(2)]

        w_full = [sem(f"w_full{s}") for s in range(R)]
        tile_done = sem("tile_done")
        acc_free = sem("acc_free")
        consts_in, x_in, mem_in = sem("consts_in"), sem("x_in"), sem("mem_in")
        zeroed = sem("zeroed")
        sq_ready, ss_ready = sem("sq_ready"), sem("ss_ready")
        root_ready, norm_ready = sem("root_ready"), sem("norm_ready")
        outs = sem("outs")
        pe_turn = sem("pe_turn")
        staged, stage_out = sem("staged"), [sem("stage_out0"), sem("stage_out1")]
        mv_full, mv_free = sem("mv_full"), sem("mv_free")

        root, _ = view(tmp, TMP_N - 2 * HN, 2, HN)
        NORMS = ["mem", "mix", "cross", "ffn", "final"]

        def norm_halves(name):
            return [(0, MEM)] if name == "mem" else [(0, HN), (HN, HN)]

        def norm_act(act, name, src, dst):
            m = NORMS.index(name)
            for c in range(4):
                nc.scalar.activation(dst[:, 4 * c:4 * c + 4, :], src[:, 4 * c:4 * c + 4, :],
                                     ACT.Square).then_inc(sq_ready, 1)
            act.wait_ge(ss_ready, m + 1)
            halves = norm_halves(name)
            nc.scalar.activation(root[:, 0:len(halves), 0:halves[0][1]],
                                 psum[:, 4:4 + len(halves), 0:halves[0][1]],
                                 ACT.Sqrt, bias=eps, scale=1.0 / D).then_inc(root_ready, 1)

        def norm_pe(pe, name, dst):
            m = NORMS.index(name)
            for c in range(4):
                pe.wait_ge(sq_ready, 4 * m + c + 1)
                for k in range(4 * c, 4 * c + 4):
                    for b, (o, w) in enumerate(norm_halves(name)):
                        mm = nc.tensor.matmul(psum[:, 4 + b, 0:w], ones, dst[:, k, o:o + w],
                                              start=(k == 0), stop=(k == KD - 1))
            mm.then_inc(ss_ready, 1)

        def norm_dve(dve, name, src, dst, gain):
            m = NORMS.index(name)
            dve.wait_ge(root_ready, m + 1)
            halves = norm_halves(name)
            w = halves[0][1]
            rt = root[:, 0:len(halves), 0:w]
            nc.vector.reciprocal(rt, rt)
            dve.drain()
            for k in range(KD):
                mul = nc.vector.scalar_tensor_tensor(
                    out=dst[:, k, :].rearrange("p (h n) -> p h n", n=w),
                    in0=src[:, k, :].rearrange("p (h n) -> p h n", n=w),
                    scalar=gain[:, k:k + 1], in1=rt, op0=ALU.mult, op1=ALU.mult)
            mul.then_inc(norm_ready, 1)

        def freed(tile):
            return tile - 2 - T_MK + 1

        def gemm_tile(pe, tile, src):
            if isinstance(tile, tuple):
                i, per, off = tile
                full, free, k0 = i * (16 * per // R) + 16 * (off // R + 1), i * per + freed(off), off
            else:
                full, free, k0 = 16 * (tile // R + 1), freed(tile), tile
            pe.wait_ge(w_full[k0 % R], full)
            pe.wait_ge(acc_free, free)
            for k in range(KD):
                for b in range(2):
                    mm = nc.tensor.matmul(acc[k0 % 2][:, b, :], ring[:, k0 % R, k * P:(k + 1) * P],
                                          src[:, k, b * HN:(b + 1) * HN], start=(k == 0), stop=(k == KD - 1))
            mm.then_inc(tile_done, 1)

        def done(off, i=None, per=None):
            return off + 1 if i is None else i * per + (off + 1)

        xp, e = view(tmp, 0, 3, 3 + NP_ + 3 + NS)
        yc, e = view(tmp, e, 3, NP_ + 3 + NS)
        cq, e = view(tmp, e, 2, NT)
        sqk, e = view(tmp, e, 2, NT)
        rqk = yc
        assert e <= TMP_N
        a_end = qkv_end
        conv_out, a_end = view(arena, a_end, HEADS, 18)
        BG = arena[0:64, a_end:a_end + NPAD]
        a_end += NPAD
        bgt = arena[0:64, a_end:a_end + NPAD]
        wba, e = view(arena, a_end + NPAD, KD, 64)
        assert e <= BIG
        raw_ready, conv_done, qk_sq, qk_ss = sem("raw_ready"), sem("conv_done"), sem("qk_sq"), sem("qk_ss")
        qk_root, qk_done = sem("qk_root"), sem("qk_done")
        ba_full, ba_free, ba_parts, ba_done, ba_in = (sem("ba_full"), sem("ba_free"), sem("ba_parts"),
                                                      sem("ba_done"), sem("ba_in"))

        e = a_end
        Sp, e = view(arena, e, HEADS, DH)
        Ss, e = view(arena, e, HEADS, DH)
        Vc, e = view(arena, e, HEADS, CH)
        assert e <= BIG
        e = BIG + HEADS * NPAD
        Kt, e = view(arena, e, HEADS, DH)
        Vt, e = view(arena, e, HEADS, DH)
        VN, e = view(arena, e, HEADS, DH)
        kd, e = view(arena, e, HEADS, DH)
        assert e <= BIG + OAB_N
        e = 0
        blk = {}
        for name in ("Kc", "Qc", "gU", "Dd", "ET", "ES", "EG", "A", "Bl", "kg", "qd", "QKT", "R"):
            blk[name], e = view(tmp, e, HEADS, CH)
        Tt, e = view(tmp, e, HEADS, CH)
        bc, e = tmp[0:64, e:e + CH], e + CH
        bg, e = tmp[0:64, e:e + CH], e + CH
        gcol, e = tmp[0:64, e:e + 8], e + 8
        ek, e = tmp[0:64, e:e + 8], e + 8
        assert e <= TMP_N, e
        Kc, Qc, gU, Dd, ET, ES, EG, A, Bl, kg, qd, QKT, Rt = (blk[n] for n in (
            "Kc", "Qc", "gU", "Dd", "ET", "ES", "EG", "A", "Bl", "kg", "qd", "QKT", "R"))
        XS, oS, sqo, rto = ES, ET, gU, Dd
        names = ("c_qb c_kv p_bg d_gu p_kt p_vt a_kvt p_kk p_g d_dd a_exp d_a p_x a_x p_rt d_r p_ks d_rr "
                 "p_vn a_vn p_o p_s d_s a_o p_oss a_rto d_o").split()
        s = {n: sem("gdn_" + n) for n in names}
        state_in = sem("state_in")
        b8 = [psum[:, i, :] for i in range(8)]

        def hc(ap, w=CH):
            return ap.rearrange("p (h c) -> p h c", c=w)

        def two(b, rows=P):
            return psum[0:rows, b:b + 2, :].rearrange("p b (h c) -> p (b h) c", c=DH)

        e = 0
        ndist, e = view(arena, e, 4, NP_)
        ndist_s, e = view(arena, e, 1, NT)
        qh, e = view(arena, e, 1, NT)
        kh, e = view(arena, e, 1, NT)
        vh, e = view(arena, e, 1, NT)
        kc, e = view(arena, e, 1, NP_)
        vc, e = view(arena, e, 4, DH)
        assert e <= KD * NT
        vt, e = view(tmp, 0, QT, DH)
        sc, e = view(tmp, e, 2, NT)
        pr, e = view(tmp, e, 1, NT)
        aT, e = view(tmp, e, 4, P)
        ob, e = view(tmp, e, 1, NT)
        osq, e = view(tmp, e, 1, NT)
        ort, e = view(tmp, e, 2, HN)
        st, e = view(tmp, e, 1, 16)
        assert e <= TMP_N
        qh, kh, vh, kc, pr, ob, osq, st = (v[:, 0, :] for v in (qh, kh, vh, kc, pr, ob, osq, st))
        ndist_s = ndist_s[:, 0, :]
        mx, zz, rz = st[:, 0:2], st[:, 2:4], st[:, 4:6]
        g_diff8 = lamb[:, 5:6]
        lam, nlam = lamb[:, 3:4], lamb[:, 4:5]
        at = {n: sem("att_" + n) for n in
              "dist_in qkv cache_in rows_out pvt vt s m e a pT aT o obs oss rt done".split()}
        lam_parts, lam_exp = sem("lam_parts"), sem("lam_exp")

        sgb, e = view(tmp, 0, 2, HN)
        t1, e = view(tmp, e, 2, HN)
        gates_ready, merged = sem("gates_ready"), sem("merged")
        x_again = sem("x_again")
        x_done = sem("x_done")

        def hregion(start, a, b):
            return view(H[:, :, :].rearrange("p a b -> p (a b)"), start, a, b)
        mkp, e = hregion(0, 4, MEM)
        mks, e = hregion(e, 4, MEM)
        mvp, e = hregion(e, 2, MD)
        mvs, e = hregion(e, 2, MD)
        qst, e = view(tmp, 0, 4, NT)
        pm, e = view(tmp, e, 4, MEM)
        pms, e = view(tmp, e, 1, MEM)
        pmT, e = view(tmp, e, 2, NP_)
        pmTs, e = view(tmp, e, 2, NS)
        mst, e = view(tmp, e, 1, 16)
        assert e <= TMP_N
        pms, mst = pms[:, 0, :], mst[:, 0, :]
        ca = {n: sem("cross_" + n) for n in
              "qfree in s m e p pT T o oev".split()}
        ca_kv = ca["in"]

        qps, e = view(tmp, 0, 4, NT)
        slotT, e = view(tmp, 2048, 3, QT * P)
        assert e == 3968
        skT, e = view(arena, KD * NT, 2 * HEADS, NKEY)
        tv, e = view(arena, e, QT, 2 * TOPK)
        tif, e = view(arena, e, QT, 2 * TOPK)
        work, e = view(arena, e, QT, NKEY)
        last, e = view(arena, e, 1, NKEY)
        last = last[:, 0, :]
        cand, e = view(arena, e, QT, TOPK * TOPK)
        cwork, e = view(arena, e, QT, TOPK * TOPK)
        bestv, e = view(arena, e, QT, TOPK)
        abf, e = view(arena, e, 2, QT * TOPK)
        eqb, e = view(arena, e, QT * TOPK, TOPK)
        zs, e = view(arena, e, 1, QT * HEADS)
        best, e = view(arena, e, QT, P)
        slots, e = view(arena, e, 3 * QT, P)
        assert e <= BIG + OAB_N, e
        tv4, tif4 = (v.rearrange("p q (s n) -> p q s n", s=2) for v in (tv, tif))
        abf, slots = abf.rearrange("p a (q n) -> p a q n", q=QT), slots.rearrange("p (j q) n -> p j q n", j=3)
        zs = zs[:, 0, :]
        tiu = ctx.enter_context(nc.sbuf_tensor("tiu", [P, QT, 2 * TOPK], U32))
        selu = ctx.enter_context(nc.sbuf_tensor("selu", [P, 3, QT, TOPK], U32))
        pk = {n: sem("peer_" + n) for n in
              "keys_in qs s sev top gexp sl slT slTe eq oh g gev".split()}
        OH = []
        for start in (0, 1024, 3968, 4992):
            oh, e = view(tmp, start, 8, P)
            OH.append(oh.rearrange("p (j n) a -> p j n a", j=2))
        assert e <= TMP_N
        stored = [sem("stored0"), sem("stored1")]
        Gs = [view(arena, KD * NT * (1 + b), P, GT)[0] for b in range(2)]
        GSTEPS = GT // 4
        NGT = NT // GT
        assert P * GT == KD * NT
        assert GSTEPS % 4 == 1 and (NT // 4) % 4 == 0

        def gate_steps(engine, g, step):
            with engine.Fori(0, GSTEPS // 4) as i:
                for b in range(4):
                    step(i * 4 + (g * GSTEPS + b), (g + b) % 4, i * 16 + 4 * b)
            step(g * GSTEPS + GSTEPS - 1, g % 4, GT - 4)

        ROW = 4
        AT_RING, AT_H, AT_M, AT_TMP = 0, R * D * ROW, (R * D + KD * NT + KD * NT) * ROW, \
            (R * D + KD * NT + BIG + OAB_N) * ROW

        def placed(name, offset, shape, dt=F32R):
            v = nc.alloc_sbuf_tensor_at(name, [P] + list(shape), dt, offset=base + offset)
            return v[tuple(slice(None) for _ in range(1 + len(shape)))]

        def as_f32(ap):
            return ap.bitcast(F32)

        h_hi = placed("h_hi", AT_M, [KD, NT])
        h_lo = placed("h_lo", AT_M + KD * NT * ROW, [KD, NT])
        GR = 2
        NG = NKEY // GR
        SLOT = D * ROW
        u_raw = [placed(f"u_raw{b}", AT_RING + 2 * b * SLOT, [D], F32) for b in range(2)]
        u_lo = [placed(f"u_lo{b}", AT_RING + 2 * b * SLOT, [D]) for b in range(2)]
        u_hi = [placed(f"u_hi{b}", AT_RING + (2 * b + 1) * SLOT, [D]) for b in range(2)]
        v_raw = placed("v_raw", AT_H, [GR, D], F32)
        v_lo = placed("v_lo", AT_H, [GR, D])
        v_hi = placed("v_hi", AT_H + GR * SLOT, [GR, D])
        assert AT_H + 2 * GR * SLOT <= AT_M - KD * NT * ROW
        CB = GR * NT * ROW
        coef_hi = [placed(f"coef_hi{b}", AT_TMP + 2 * b * CB, [GR, NT]) for b in range(2)]
        coef_lo = [placed(f"coef_lo{b}", AT_TMP + (2 * b + 1) * CB, [GR, NT]) for b in range(2)]
        gat = [placed(f"gat{b}", AT_TMP + (4 + b) * CB, [GR, NT], F32) for b in range(2)]
        hid = placed("hid", AT_TMP + 6 * CB, [2, NT], F32)
        assert 6 * CB + 2 * NT * ROW <= TMP_N * ROW
        VHALF = [slice(0, D // 2), slice(D // 2, D)]
        u_in, v_in, g_full = [sem("u_in0"), sem("u_in1")], [sem("v_in0"), sem("v_in1")], [sem("g_full0"), sem("g_full1")]
        h_rounded, h_split = sem("h_rounded"), sem("h_split")
        u_rounded, u_split, u_done = sem("u_rounded"), sem("u_split"), sem("u_done")
        v_rounded, v_split, v_done = sem("v_rounded"), sem("v_split"), sem("v_done")
        hid_ready, hid_free, coef_ready = sem("hid_ready"), sem("hid_free"), sem("coef_ready")
        y_full, y_free = sem("y_full"), sem("y_free")
        y_out = sem("y_out")

        def upto(count, reg=None, per=0):
            return count if reg is None else reg * per + count

        block = ctx.enter_context(nc.Block())

        @block.sync
        def _(sp):
            sp.dma_start(const[:, :], t["consts"]).then_inc(consts_in, 16)
            sp.dma_start(small[:, :], t["small"]).then_inc(consts_in, 16)
            sp.dma_start(memT, t["memT"]).then_inc(mem_in, 16)
            for k in range(R):
                sp.dma_start(ring[:, k, :], t["weights"][k]).then_inc(w_full[k], 16)
            sp.dma_start(X, t["xT"]).then_inc(x_in, 16)
            sp.dma_start(wba, t["w_ba"]).then_inc(ba_in, 16)
            with sp.Fori(1, N_STREAM // R) as i:
                for k in range(R):
                    src = t["weights"][bass.ds(i * R + k, 1)].rearrange("o p n -> p (o n)")
                    sp.wait_ge(tile_done, i * R + (k - R + 1))
                    sp.dma_start(ring[:, k, :], src).then_inc(w_full[k], 16)

            def load_u(group, reg=None):
                for k in range(GR):
                    n = group * GR + k
                    src = t["uT"][n] if reg is None else \
                        t["uT"][bass.ds(reg * (2 * GR) + n, 1)].rearrange("o p n -> p (o n)")
                    if n >= 2:
                        sp.wait_ge(u_done, upto(n - 1, reg, 2 * GR))
                    sp.dma_start(u_raw[k], src).then_inc(u_in[k], 16)

            def load_v(group, reg=None):
                src = t["v"][group * GR:(group + 1) * GR] if reg is None else \
                    t["v"][bass.ds(reg * (2 * GR) + group * GR, GR)]
                for e in range(2):
                    if group >= 1:
                        sp.wait_ge(y_full, upto((group - 1) * KD + KD // 2 * (e + 1), reg, 2 * KD))
                    sp.dma_start(v_raw[:, :, VHALF[e]], src[:, :, VHALF[e]].rearrange("r p n -> p r n"))\
                        .then_inc(v_in[e], 16)

            sp.wait_ge(tile_done, N_STREAM)
            load_u(0)
            for g in range(NGT):
                sp.wait_ge(pk["gev"], (g + 1) * GSTEPS + 4)
                sp.dma_start(t["gates"][g], Gs[g % 2]).then_inc(stored[g % 2], 16)
            sp.wait_ge(h_split, 1)
            load_u(1)
            load_v(0)
            with sp.Fori(0, NG // 2 - 1) as i:
                for g in range(2):
                    load_u(g + 2, i)
                    load_v(g + 1, i)
            load_v(NG - 1)
            sp.wait_ge(norm_ready, len(NORMS))
            sp.dma_start(t["y"], H[:, :, :]).then_inc(y_out, 16)
            sp.wait_ge(y_out, 16)

        @block.gpsimd
        def _(pool):
            nc.gpsimd.memset(xp[:, :, 0:3], 0.0).then_inc(zeroed, 1)
            for g in range(4):
                pool.wait_ge(staged, g + 1)
                pool.dma_start(t["mem_v"][:, :, g * 512:(g + 1) * 512], stage[g % 2]).then_inc(stage_out[g % 2], 16)
            for k in range(KD):
                pool.wait_ge(staged, 4 + k + 1)
                pool.dma_start(t["mem_k"][k], stage[k % 2][:, 0, 0:MEM]).then_inc(stage_out[k % 2], 16)
            pool.wait_ge(norm_ready, 2)
            nc.gpsimd.memset(QKV[:, :, NT:NPAD], 0.0)
            nc.gpsimd.memset(OA[:, :, NT:NPAD], 0.0)
            nc.gpsimd.memset(BG, 0.0)
            pool.drain().then_inc(zeroed, 1)
            pool.wait_ge(ba_done, 1)
            nc.gpsimd.memset(Sp, 0.0).then_inc(zeroed, 1)
            pool.dma_start(Ss, t["state_in"]).then_inc(state_in, 16)
            pool.wait_ge(conv_done, 3 * HEADS)
            pool.wait_ge(qk_done, HEADS)
            pool.dma_start(t["conv_state"], conv_out).then_inc(outs, 16)
            pool.wait_ge(s["d_s"], NCH)
            pool.dma_start(t["state_p"], Sp).then_inc(outs, 16)
            pool.wait_ge(s["d_s"], NCH + 1)
            pool.dma_start(t["state_s"], Ss).then_inc(outs, 16)
            pool.wait_ge(s["d_o"], NCH + 1)
            pool.wait_ge(outs, 48)
            pool.dma_start(ndist, t["ndist"]).then_inc(at["dist_in"], 16)
            pool.dma_start(ndist_s[0:NS, :], t["ndist_s"]).then_inc(at["dist_in"], 16)
            pool.dma_start(kc, t["cache_k"][0]).then_inc(at["cache_in"], 16)
            pool.dma_start(vc, t["cache_v"][0]).then_inc(at["cache_in"], 16)

            def rows_out(h, k_dst, v_dst):
                pool.wait_ge(at["qkv"], h * 3 + 3)
                pool.dma_start(k_dst, kh).then_inc(at["rows_out"], 16)
                pool.dma_start(v_dst, vh).then_inc(at["rows_out"], 16)

            with pool.Fori(0, HEADS - 1) as h:
                k_dst = t["k_rows"][bass.ds(h, 1)].rearrange("o p n -> p (o n)")
                v_dst = t["v_rows"][bass.ds(h, 1)].rearrange("o p n -> p (o n)")
                k_src = t["cache_k"][bass.ds(h + 1, 1)].rearrange("o p n -> p (o n)")
                v_src = t["cache_v"][bass.ds(h + 1, 1)].rearrange("o p b n -> p (o b) n")
                rows_out(h, k_dst, v_dst)
                pool.wait_ge(at["o"], h * 5 + 5)
                pool.dma_start(kc, k_src).then_inc(at["cache_in"], 16)
                pool.dma_start(vc, v_src).then_inc(at["cache_in"], 16)
            rows_out(HEADS - 1, t["k_rows"][HEADS - 1], t["v_rows"][HEADS - 1])
            pool.wait_ge(at["done"], HEADS)
            pool.wait_ge(at["rows_out"], 32 * HEADS)
            pool.dma_start(X, t["xT"]).then_inc(x_again, 16)
            for b in range(2):
                pool.wait_ge(stage_out[b], 16 * 10)
            with pool.Fori(0, MH) as h:
                srcs = [t["mem_k"][bass.ds(h * 4, 4)].rearrange("c p n -> p c n"),
                        t["cmem_k"][bass.ds(h * 4, 4)].rearrange("c p n -> p c n"),
                        t["mem_v"][:, :, bass.ds(h * MD, MD)],
                        t["cmem_v"][:, :, bass.ds(h * MD, MD)]]
                pool.wait_ge(ca["qfree"], h + 1)
                for dst, src in zip((mkp, mks, mvp, mvs), srcs):
                    pool.dma_start(dst, src).then_inc(ca_kv, 16)
            pool.wait_ge(x_done, 2)
            pool.dma_start(skT, t["sub_keys"]).then_inc(pk["keys_in"], 16)
            for g in range(NGT):
                def step(n, b, col):
                    gate = slotT[:, 2, bass.ds(n * 4, 4)].unsqueeze(2).to_broadcast([P, 4, P])
                    pool.wait_ge(pk["eq"], n + 1)
                    nc.gpsimd.tensor_tensor(OH[b][:, 0], OH[b][:, 0], gate, ALU.mult).then_inc(pk["oh"], 1)
                gate_steps(pool, g, step)
            for b in range(2):
                pool.wait_ge(stored[b], 16 * (NGT // 2))
            pool.wait_ge(pk["gev"], NT // 4 + 4)

            def load_gates(b, src):
                dst = gat[b].rearrange("p r (t n) -> p r t n", t=NGT)
                for k in range(GR):
                    pool.dma_start(dst[:, k], src[:, :, k, :].rearrange("t p n -> p t n")).then_inc(g_full[b], 16)

            for g in range(2):
                load_gates(g, t["gates"][:, :, GR * g:GR * g + GR, :])
            with pool.Fori(0, NG // 2 - 1) as i:
                for b in range(2):
                    src = t["gates"][:, :, bass.ds(i * (2 * GR) + GR * (2 + b), GR), :]
                    pool.wait_ge(coef_ready, i * (2 * GR) + GR * (b + 1))
                    load_gates(b, src)

        @block.tensor
        def _(pe):
            pe.wait_ge(consts_in, 32)

            def wait_first(semaphore, value):
                pe.wait_ge(semaphore, value)
                pe.sem_inc(pe_turn, 1)

            norm_pe(pe, "mem", hmT)
            pe.wait_ge(norm_ready, 1)
            for g in range(4):
                if g >= 2:
                    pe.wait_ge(mv_free, g - 1)
                for kq in range(4):
                    tile = T_MV + 4 * g + kq
                    pe.wait_ge(w_full[tile % R], 16 * (tile // R + 1))
                    for k in range(4):
                        for m in range(2):
                            mm = nc.tensor.matmul(psum[:, 2 * (g % 2) + m, :],
                                                  hmT[:, 4 * kq + k, m * P:(m + 1) * P],
                                                  ring[:, tile % R, k * 512:(k + 1) * 512],
                                                  start=(kq == 0 and k == 0), stop=(kq == 3 and k == 3))
                    mm.then_inc(tile_done, 1)
            pe.wait_ge(mv_free, 4)
            for n in range(KD):
                tile = T_MK + n
                pe.wait_ge(w_full[tile % R], 16 * (tile // R + 1))
                if n >= 2:
                    pe.wait_ge(acc_free, n - 1)
                for k in range(KD):
                    mm = nc.tensor.matmul(psum[:, 2 * (n % 2), 0:MEM], ring[:, tile % R, k * P:(k + 1) * P],
                                          hmT[:, k, :], start=(k == 0), stop=(k == KD - 1))
                mm.then_inc(tile_done, 1)

            norm_pe(pe, "mix", H)
            pe.wait_ge(norm_ready, 2)
            pe.wait_ge(ba_in, 16)
            for k in range(KD):
                for b in range(2):
                    mm = nc.tensor.matmul(psum[0:64, 6 + b, 0:HN], wba[:, k, :], H[:, k, b * HN:(b + 1) * HN],
                                          start=(k == 0), stop=(k == KD - 1))
            mm.then_inc(ba_full, 1)
            pe.wait_ge(ba_free, 1)
            with pe.Fori(0, HEADS) as i:
                for j in range(4):
                    gemm_tile(pe, (i, 4, T_GDN + j), H)
                pe.wait_ge(qk_sq, i * 2 + 2)
                for j in range(2):
                    for b in range(2):
                        mm = nc.tensor.matmul(aux[j][:, b, :], ones, sqk[:, j, b * HN:(b + 1) * HN],
                                              start=True, stop=True)
                mm.then_inc(qk_ss, 1)

            def gdn_block(c, S):
                one = c + 1
                wait_first(s["c_qb"], one)
                nc.tensor.transpose(b8[0][0:64, 0:64], bc, ident[0:64, 0:64]).then_inc(s["p_bg"], 1)
                wait_first(s["c_kv"], one)
                for h in range(HEADS):
                    mm = nc.tensor.transpose(two(4, CH)[:, h, :], Kc[:, h, :], ident)
                mm.then_inc(s["p_kt"], 1)
                for h in range(HEADS):
                    mm = nc.tensor.transpose(two(6, CH)[:, h, :], Vc[:, h, :], ident)
                mm.then_inc(s["p_vt"], 1)
                for h in range(HEADS):
                    nc.tensor.matmul(hc(b8[2])[0:CH, h, :], Kc[:, h, :], Kc[:, h, :], start=True, stop=True)
                    mm = nc.tensor.matmul(hc(b8[3])[0:CH, h, :], Kc[:, h, :], Qc[:, h, :], start=True, stop=True)
                mm.then_inc(s["p_kk"], 1)
                wait_first(s["d_gu"], one)
                nc.tensor.matmul(b8[0][0:CH, 64:72], cst("upper", CH), bg[:, 32:40], start=True, stop=True)
                nc.tensor.matmul(b8[1], ones[0:CH, :], gU[0:CH, :, :], start=True, stop=True)\
                    .then_inc(s["p_g"], 1)
                wait_first(s["d_a"], one)
                for h in range(HEADS):
                    mm = nc.tensor.matmul(hc(b8[0])[0:CH, h, :], Bl[0:CH, h, :], ident[0:CH, 0:CH],
                                          start=True, stop=True)
                mm.then_inc(s["p_x"], 1)
                for lv in range(1, LEVELS):
                    wait_first(s["d_r"], c * LEVELS + lv)
                    for h in range(HEADS):
                        mm = nc.tensor.matmul(hc(b8[0])[0:CH, h, :], Bl[0:CH, h, :], Rt[0:CH, h, :],
                                              start=True, stop=True)
                    mm.then_inc(s["p_x"], 1)
                    wait_first(s["a_x"], c * (LEVELS - 1) + lv)
                    for h in range(HEADS):
                        nc.tensor.matmul(hc(b8[1])[0:CH, h, :], Tt[0:CH, h, :], XS[0:CH, h, :],
                                         start=True, stop=True)
                    for h in range(HEADS):
                        mm = nc.tensor.matmul(hc(b8[2])[0:CH, h, :], XS[0:CH, h, :], Tt[0:CH, h, :],
                                              start=True, stop=True)
                    mm.then_inc(s["p_rt"], 1)
                pe.wait_ge(s["a_kvt"], c * 2 + 2)
                for h in range(HEADS):
                    mm = nc.tensor.matmul(two(4, CH)[:, h, :], kg[:, h, :], S[:, h, :], start=True, stop=True)
                mm.then_inc(s["p_ks"], 1)
                wait_first(s["d_rr"], one)
                for h in range(HEADS):
                    mm = nc.tensor.matmul(two(6, CH)[:, h, :], Rt[0:CH, h, :], Vt[0:CH, h, :],
                                          start=True, stop=True)
                mm.then_inc(s["p_vn"], 1)
                wait_first(s["a_vn"], one)
                for h in range(HEADS):
                    nc.tensor.matmul(hc(b8[3])[:, h, :], S[:, h, :], qd[:, h, :], start=True, stop=False)
                    mm = nc.tensor.matmul(hc(b8[3])[:, h, :], VN[0:CH, h, :], QKT[0:CH, h, :],
                                          start=False, stop=True)
                mm.then_inc(s["p_o"], 1)
                for h in range(HEADS):
                    mm = nc.tensor.matmul(two(4)[:, h, :], kd[0:CH, h, :], VN[0:CH, h, :],
                                          start=True, stop=True)
                mm.then_inc(s["p_s"], 1)
                pe.wait_ge(s["a_o"], one)
                nc.tensor.matmul(b8[1], ones, sqo, start=True, stop=True).then_inc(s["p_oss"], 1)

            pe.wait_ge(qk_done, HEADS)
            pe.wait_ge(acc_free, freed(T_DIFF + 1))
            with pe.Fori(0, NCH) as c:
                gdn_block(c, Sp)
            pe.wait_ge(state_in, 16)
            gdn_block(NCH, Ss)
            pe.wait_ge(s["d_o"], NCH + 1)

            with pe.Fori(0, HEADS) as h:
                for j in range(4):
                    gemm_tile(pe, (h, 4, T_DIFF + j), H)
                pe.wait_ge(at["qkv"], h * 3 + 3)
                for b in range(4):
                    nc.tensor.transpose(psum[:, 6, b * P:(b + 1) * P], vh[:, b * P:(b + 1) * P], ident)
                nc.tensor.transpose(psum[0:NS, 7, 0:P], vh[:, NP_:NT], ident).then_inc(at["pvt"], 1)
                for q in range(QT):
                    if q == 0:
                        wait_first(at["vt"], h + 1)
                    else:
                        wait_first(at["m"], h * 10 + 2 * q)
                    if q == 4:
                        wait_first(at["cache_in"], h * 32 + 32)
                        wait_first(at["obs"], h * 2 + 1)
                    for m in range(2):
                        r = slice(64 * m, 64 * m + 64)
                        if q < 4:
                            mm = nc.tensor.matmul(psum[:, 4 + m, 0:P * (q + 1)], qh[r, q * P:(q + 1) * P],
                                                  kh[r, 0:P * (q + 1)], start=True, stop=True)
                        else:
                            nc.tensor.matmul(psum[0:NS, 4 + m, :], qh[r, NP_:NT], kc[r, :], start=True, stop=True)
                            mm = nc.tensor.matmul(psum[0:NS, 7 - m, 64 * m:64 * m + NS], qh[r, NP_:NT],
                                                  kh[r, NP_:NT], start=True, stop=True)
                        mm.then_inc(at["s"], 1)
                    wait_first(at["a"], h * 5 + q + 1)
                    if q < 4:
                        for b in range(q + 1):
                            mm = nc.tensor.transpose(psum[:, 6, b * P:(b + 1) * P], pr[:, b * P:(b + 1) * P], ident)
                    else:
                        nc.tensor.transpose(psum[0:NS, 6, P:P + NS], pr[0:NS, NP_:NT], ident[0:NS, 0:NS])
                        for b in range(4):
                            mm = nc.tensor.transpose(psum[:, 6, b * NS:(b + 1) * NS], pr[0:NS, b * P:(b + 1) * P],
                                                     ident[0:NS, 0:NS])
                    mm.then_inc(at["pT"], 1)
                    wait_first(at["aT"], h * 5 + q + 1)
                    if q < 4:
                        for b in range(q + 1):
                            mm = nc.tensor.matmul(psum[:, 7, q * P:(q + 1) * P], vt[:, b, :], aT[:, b, :],
                                                  start=(b == 0), stop=(b == q))
                    else:
                        for b in range(4):
                            nc.tensor.matmul(psum[:, 7, 0:NS], vc[:, b, :], aT[:, 0, b * NS:(b + 1) * NS],
                                             start=(b == 0), stop=False)
                        mm = nc.tensor.matmul(psum[:, 7, 0:NS], vt[0:NS, 4, :], aT[0:NS, 1, 0:NS],
                                              start=False, stop=True)
                    mm.then_inc(at["o"], 1)
                wait_first(at["obs"], h * 2 + 2)
                for b in range(2):
                    mm = nc.tensor.matmul(psum[:, 4 + b, 0:HN], ones, osq[:, b * HN:(b + 1) * HN],
                                          start=True, stop=True)
                mm.then_inc(at["oss"], 1)
            pe.wait_ge(at["done"], HEADS)

            with pe.Fori(0, 2) as i:
                for k in range(4):
                    gemm_tile(pe, (i, 4, T_GATE + k), H)
            with pe.Fori(0, 8) as i:
                for d in range(2):
                    gemm_tile(pe, (i, 4, T_MERGE + 2 * d), H)
                    tile = T_MERGE + 2 * d + 1
                    pe.wait_ge(w_full[tile % R], i * 16 + 16 * (tile // R + 1))
                    pe.wait_ge(acc_free, i * 4 + freed(tile))
                    pe.wait_ge(merged, i * 2 + (d + 1))
                    for k in range(HEADS):
                        for b in range(2):
                            nc.tensor.matmul(acc[1][:, b, :], ring[:, tile % R, k * P:(k + 1) * P],
                                             OA[:, k, b * HN:(b + 1) * HN],
                                             start=(k == 0), stop=(k == HEADS - 1))
                    for k in range(HEADS):
                        for b in range(2):
                            mm = nc.tensor.matmul(aux[d % 2][:, b, :],
                                                  ring[:, tile % R, (HEADS + k) * P:(HEADS + k + 1) * P],
                                                  OB[:, k, b * HN:(b + 1) * HN],
                                                  start=(k == 0), stop=(k == HEADS - 1))
                    mm.then_inc(tile_done, 1)
            pe.wait_ge(merged, 17)
            with pe.Fori(0, 4) as i:
                for k in range(4):
                    gemm_tile(pe, (i, 4, T_OUT + k), M)
            norm_pe(pe, "cross", H)
            pe.wait_ge(norm_ready, 3)

            with pe.Fori(0, 4) as i:
                for k in range(4):
                    gemm_tile(pe, (i, 4, T_MQ + k), H)
            pe.drain().then_inc(ca["qfree"], 1)
            with pe.Fori(0, MH) as h:
                pe.wait_ge(ca_kv, h * 64 + 64)
                pe.wait_ge(ca["T"], h * 3 + 1)
                for q in range(4):
                    for k in range(4):
                        mm = nc.tensor.matmul(psum[:, 4 + q // 2, (q % 2) * MEM:(q % 2 + 1) * MEM],
                                              qst[:, k, q * P:(q + 1) * P], mkp[:, k, :],
                                              start=(k == 0), stop=(k == 3))
                mm.then_inc(ca["s"], 1)
                for k in range(4):
                    mm = nc.tensor.matmul(psum[0:NS, 6, 0:MEM], qst[:, k, NP_:NT], mks[:, k, :],
                                          start=(k == 0), stop=(k == 3))
                mm.then_inc(ca["s"], 1)
                wait_first(ca["p"], h * 2 + 1)
                for b in range(2):
                    for q in range(4):
                        mm = nc.tensor.transpose(psum[:, 4 + b, q * P:(q + 1) * P], pm[:, q, b * P:(b + 1) * P], ident)
                mm.then_inc(ca["pT"], 1)
                wait_first(ca["p"], h * 2 + 2)
                for b in range(2):
                    mm = nc.tensor.transpose(psum[:, 6, b * NS:(b + 1) * NS], pms[0:NS, b * P:(b + 1) * P],
                                             ident[0:NS, 0:NS])
                mm.then_inc(ca["pT"], 1)
                pe.wait_ge(ca["T"], h * 3 + 3)
                for k in range(4):
                    pe.wait_ge(ca["oev"], h * 4 + (k + 1))
                    for b in range(2):
                        nc.tensor.matmul(psum[:, 2 * (k % 2), :], mvp[:, b, k * P:(k + 1) * P], pmT[:, b, :],
                                         start=(b == 0), stop=(b == 1))
                    for b in range(2):
                        mm = nc.tensor.matmul(psum[:, 2 * (k % 2) + 1, 0:NS], mvs[:, b, k * P:(k + 1) * P],
                                              pmTs[:, b, :], start=(b == 0), stop=(b == 1))
                    mm.then_inc(ca["o"], 1)
                pe.drain().then_inc(ca["qfree"], 1)
            pe.wait_ge(ca["oev"], 2 + 16)
            with pe.Fori(0, 4) as i:
                for k in range(4):
                    gemm_tile(pe, (i, 4, T_MO + k), OC)
            norm_pe(pe, "ffn", H)
            pe.wait_ge(norm_ready, 4)

            pe.wait_ge(pk["keys_in"], 16)
            with pe.Fori(0, 4) as i:
                for k in range(4):
                    gemm_tile(pe, (i, 4, T_PQ + k), H)
                    pe.wait_ge(pk["qs"], i * 4 + k + 1)
                    key = skT[:, bass.ds(i * 4 + k, 1), :].rearrange("p o n -> p (o n)")
                    b = 4 + 2 * (k % 2)
                    pe.wait_ge(pk["sev"], i * 4 + (k + 1))
                    for q in range(QT):
                        rows = P if q < 4 else NS
                        out = psum[0:rows, b + q // 4, (q % 4) * P:(q % 4 + 1) * P]
                        mm = nc.tensor.matmul(out, qps[:, k, q * P:q * P + rows], key, start=True, stop=True)
                    mm.then_inc(pk["s"], 1)
            pe.wait_ge(pk["sl"], 1)
            for j in range(3):
                for q in range(QT):
                    out = psum[:, 4 + j, q * P:(q + 1) * P] if q < 4 else psum[:, 7, j * P:(j + 1) * P]
                    mm = nc.tensor.transpose(out, slots[:, j, q, :], ident)
            mm.then_inc(pk["slT"], 1)
            with pe.Fori(0, NT // 16) as i:
                for b in range(4):
                    pe.wait_ge(pk["oh"], i * 4 + (b + 1))
                    for n in range(4):
                        mm = nc.tensor.matmul(psum[:, 4 + b, n * P:(n + 1) * P], OH[b][:, 1, n], OH[b][:, 0, n],
                                              start=True, stop=True)
                    mm.then_inc(pk["g"], 1)

            def expert_u(group, reg=None):
                for k in range(GR):
                    n = group * GR + k
                    pe.wait_ge(u_split, upto(n + 1, reg, 2 * GR))
                    pe.wait_ge(acc_free, upto(freed(T_U + n), reg, 2 * GR))
                    for c in range(KD):
                        w_hi, w_lo = u_hi[k][:, c * P:(c + 1) * P], u_lo[k][:, c * P:(c + 1) * P]
                        for j, (w, h) in enumerate(((w_hi, h_hi), (w_hi, h_lo), (w_lo, h_hi))):
                            for b in range(2):
                                mm = nc.tensor.matmul(acc[k][:, b, :], w, h[:, c, b * HN:(b + 1) * HN],
                                                      start=(c == 0 and j == 0), stop=(c == KD - 1 and j == 2))
                    mm.then_inc(u_done, 1)

            def expert_v(group, reg=None):
                pe.wait_ge(coef_ready, upto(GR * (group + 1), reg, 2 * GR))
                c_hi, c_lo = coef_hi[group % 2], coef_lo[group % 2]
                for d in range(KD):
                    if d % (KD // 2) == 0:
                        pe.wait_ge(v_split, upto(2 * group + 2 * d // KD + 1, reg, 4))
                    pe.wait_ge(y_free, upto(group * KD + d + 1, reg, 2 * KD))
                    for k in range(GR):
                        w_hi, w_lo = v_hi[:, k, d * P:(d + 1) * P], v_lo[:, k, d * P:(d + 1) * P]
                        for j, (w, c) in enumerate(((w_hi, c_hi), (w_hi, c_lo), (w_lo, c_hi))):
                            for b in range(2):
                                mm = nc.tensor.matmul(aux[d % 2][:, b, :], w, c[:, k, b * HN:(b + 1) * HN],
                                                      start=(k == 0 and j == 0), stop=(k == GR - 1 and j == 2))
                    mm.then_inc(y_full, 1)
                pe.drain().then_inc(v_done, 1)

            pe.sem_inc(v_done, 2)
            pe.wait_ge(pk["gev"], NT // 4 + 4)
            pe.wait_ge(h_split, 1)
            expert_u(0)
            with pe.Fori(0, NG // 2 - 1) as i:
                expert_u(1, i)
                expert_v(0, i)
                expert_u(2, i)
                expert_v(1, i)
            expert_u(NG - 1)
            expert_v(NG - 2)
            expert_v(NG - 1)
            norm_pe(pe, "final", H)

        @block.scalar
        def _(act):
            act.wait_ge(consts_in, 32)
            act.wait_ge(mem_in, 16)
            norm_act(act, "mem", memT, hmT)
            for g in range(4):
                act.wait_ge(tile_done, T_MV + 4 * g + 4)
                if g >= 2:
                    act.wait_ge(stage_out[g % 2], 16)
                nc.scalar.activation(stage[g % 2], psum[:, 2 * (g % 2):2 * (g % 2) + 2, :], ACT.Copy)\
                    .then_inc(mv_free, 1)
                act.drain().then_inc(staged, 1)
            for n in range(KD):
                act.wait_ge(tile_done, T_MK + n + 1)
                act.wait_ge(stage_out[n % 2], 16 * (2 + n // 2))
                nc.scalar.activation(stage[n % 2][:, 0, 0:MEM], psum[:, 2 * (n % 2), 0:MEM], ACT.Copy)\
                    .then_inc(acc_free, 1)
                act.drain().then_inc(staged, 1)
            act.wait_ge(x_in, 16)
            norm_act(act, "mix", X, H)
            act.wait_ge(lam_parts, 1)
            nc.scalar.activation(lamb[:, 2:4], lamb[:, 0:2], ACT.Exp).then_inc(lam_exp, 1)
            act.wait_ge(ba_full, 1)
            act.wait_ge(zeroed, 2)
            ba = psum[:, 6:8, 0:HN]

            def halves(ap):
                return ap.rearrange("p (h n) -> p h n", n=HN)
            bgw = BG[:, 0:NT]
            dt, al = sml("dt_bias")[32:40, :], sml("a_log")[32:40, :]
            nc.scalar.activation(halves(bgw[0:8, :]), ba[0:8], ACT.Sigmoid)
            nc.scalar.activation(halves(bgt[32:40, 0:NT]), ba[32:40], ACT.Abs, bias=dt)
            nc.scalar.activation(halves(bgw[32:40, :]), ba[32:40], ACT.Relu, bias=dt).then_inc(ba_free, 1)
            act.drain()
            nc.scalar.activation(bgt[32:40, 0:NT], bgt[32:40, 0:NT], ACT.Exp, scale=-1.0)
            nc.scalar.activation(lamb[32:40, 6:7], al, ACT.Exp)
            act.drain()
            nc.scalar.activation(bgt[32:40, 0:NT], bgt[32:40, 0:NT], ACT.Ln, bias=1.0).then_inc(ba_parts, 1)

            state = sml("conv_state").rearrange("p (c n) -> p c n", n=3)
            act.wait_ge(zeroed, 1)
            with act.Fori(0, HEADS) as i:
                for j in range(3):
                    tail = state[:, bass.ds(i * 3 + j, 1), :].rearrange("p o n -> p (o n)")
                    act.wait_ge(tile_done, done(T_GDN + j, i, 4))
                    a = acc[(T_GDN + j) % 2]
                    nc.scalar.activation(xp[:, j, 3 + NP_:6 + NP_], tail, ACT.Copy)
                    nc.scalar.activation(xp[:, j, 3:3 + HN], a[:, 0, :], ACT.Copy)
                    nc.scalar.activation(xp[:, j, 3 + HN:3 + NP_], a[:, 1, 0:NP_ - HN], ACT.Copy)
                    nc.scalar.activation(xp[:, j, 6 + NP_:6 + NT], a[:, 1, NP_ - HN:HN], ACT.Copy)\
                        .then_inc(acc_free, 1)
                    act.drain().then_inc(raw_ready, 1)
                    act.wait_ge(conv_done, i * 3 + (j + 1))
                    if j < 2:
                        nc.scalar.activation(cq[:, j, 0:NP_], yc[:, j, 0:NP_], ACT.Silu)
                        nc.scalar.activation(cq[:, j, NP_:NT], yc[:, j, NP_ + 3:], ACT.Silu)
                        act.drain()
                        nc.scalar.activation(sqk[:, j, :], cq[:, j, :], ACT.Square).then_inc(qk_sq, 1)
                    else:
                        v = QKV[:, bass.ds(i + 2 * HEADS, 1), :].rearrange("p o n -> p (o n)")
                        nc.scalar.activation(v[:, 0:NP_], yc[:, j, 0:NP_], ACT.Silu)
                        nc.scalar.activation(v[:, NP_:NT], yc[:, j, NP_ + 3:], ACT.Silu)
                z = OA[:, bass.ds(i, 1), 0:NT].rearrange("p o (h n) -> p (o h) n", n=HN)
                act.wait_ge(tile_done, done(T_GDN + 3, i, 4))
                nc.scalar.activation(z, acc[1], ACT.Silu).then_inc(acc_free, 1)
                act.wait_ge(qk_ss, i + 1)
                for j in range(2):
                    sq = nc.scalar.activation(halves(rqk[:, j, 0:NT]), aux[j], ACT.Sqrt, bias=eps)
                sq.then_inc(qk_root, 1)

            def gdn_block(c, dyn):
                one = c + 1
                nc.scalar.activation(Qc, QKV[:, 0:HEADS, dyn], ACT.Copy)
                nc.scalar.activation(bc, BG[:, dyn], ACT.Copy).then_inc(s["c_qb"], 1)
                act.wait_ge(s["p_kt"], one)
                nc.scalar.activation(Kt[0:CH], two(4, CH), ACT.Copy).then_inc(s["a_kvt"], 1)
                act.wait_ge(s["p_vt"], one)
                nc.scalar.activation(Vt[0:CH], two(6, CH), ACT.Copy).then_inc(s["a_kvt"], 1)
                act.wait_ge(s["d_dd"], one)
                nc.scalar.activation(ET[0:CH], ET[0:CH], ACT.Exp)
                nc.scalar.activation(ES[0:CH], ES[0:CH], ACT.Exp)
                nc.scalar.activation(ek.unsqueeze(2), Dd[0:CH, :, CH - 1:CH], ACT.Exp)
                nc.scalar.activation(EG, hc(b8[1]), ACT.Exp).then_inc(s["a_exp"], 1)
                for lv in range(1, LEVELS):
                    act.wait_ge(s["p_x"], c * LEVELS + (lv + 1))
                    nc.scalar.activation(XS[0:CH], hc(b8[0])[0:CH], ACT.Copy).then_inc(s["a_x"], 1)
                act.wait_ge(s["p_vn"], one)
                nc.scalar.activation(VN[0:CH], two(6, CH), ACT.Copy).then_inc(s["a_vn"], 1)
                act.wait_ge(s["p_o"], one)
                nc.scalar.activation(sqo, hc(b8[3]), ACT.Square).then_inc(s["a_o"], 1)
                nc.scalar.activation(oS, hc(b8[3]), ACT.Copy)
                act.wait_ge(s["p_oss"], one)
                nc.scalar.activation(rto, hc(b8[1]), ACT.Sqrt, bias=eps, scale=1.0 / DH).then_inc(s["a_rto"], 1)

            act.wait_ge(ba_done, 1)
            act.wait_ge(qk_done, HEADS)
            with act.Fori(0, NCH) as c:
                gdn_block(c, bass.ds(c * CH, CH))
            gdn_block(NCH, slice(NP_, NPAD))

            act.wait_ge(s["d_o"], NCH + 1)
            act.wait_ge(outs, 48)
            with act.Fori(0, HEADS) as h:
                for j, (dst, scale) in enumerate(((qh, 0.125), (kh, 1.0), (vh, 1.0))):
                    act.wait_ge(tile_done, done(T_DIFF + j, h, 4))
                    nc.scalar.activation(halves(dst), acc[j % 2], ACT.Copy, scale=scale).then_inc(acc_free, 1)
                    act.drain().then_inc(at["qkv"], 1)
                act.wait_ge(tile_done, done(T_DIFF + 3, h, 4))
                gate = M[:, bass.ds(h, 1), :].rearrange("p o (h n) -> p (o h) n", n=HN)
                nc.scalar.activation(gate, acc[1], ACT.Sigmoid).then_inc(acc_free, 1)
                act.wait_ge(at["pvt"], h + 1)
                nc.scalar.activation(vt[:, 0:4, :], psum[:, 6, :].rearrange("p (b n) -> p b n", b=4), ACT.Copy)
                nc.scalar.activation(vt[0:NS, 4, :], psum[0:NS, 7, 0:P], ACT.Copy).then_inc(at["vt"], 1)
                for q in range(QT):
                    w = P * (q + 1) if q < 4 else NT
                    rows = P if q < 4 else NS
                    for m in range(2):
                        act.wait_ge(at["m"], h * 10 + (2 * q + m + 1))
                        nc.scalar.activation(sc[0:rows, m, 0:w], sc[0:rows, m, 0:w], ACT.Exp,
                                             bias=mx[0:rows, m:m + 1], accum_out=zz[0:rows, m:m + 1])\
                            .then_inc(at["e"], 1)
                    act.wait_ge(at["pT"], h * 5 + q + 1)
                    if q < 4:
                        nc.scalar.activation(aT[:, 0:q + 1, :],
                                             psum[:, 6, 0:w].rearrange("p (b n) -> p b n", n=P),
                                             ACT.Copy).then_inc(at["aT"], 1)
                    else:
                        nc.scalar.activation(aT[0:NS, 1, 0:NS], psum[0:NS, 6, P:P + NS], ACT.Copy)
                        nc.scalar.activation(aT[:, 0, :], psum[:, 6, 0:P], ACT.Copy).then_inc(at["aT"], 1)
                    if q == 3:
                        act.wait_ge(at["o"], h * 5 + 4)
                        nc.scalar.activation(ob[:, 0:NP_], psum[:, 7, :], ACT.Copy)
                        act.drain()
                        nc.scalar.activation(osq[:, 0:NP_], ob[:, 0:NP_], ACT.Square).then_inc(at["obs"], 1)
                act.wait_ge(at["o"], h * 5 + 5)
                nc.scalar.activation(ob[:, NP_:NT], psum[:, 7, 0:NS], ACT.Copy)
                act.drain()
                nc.scalar.activation(osq[:, NP_:NT], ob[:, NP_:NT], ACT.Square).then_inc(at["obs"], 1)
                act.wait_ge(at["oss"], h + 1)
                nc.scalar.activation(ort, aux[0], ACT.Sqrt, bias=eps, scale=1.0 / DH).then_inc(at["rt"], 1)
                act.wait_ge(at["rows_out"], h * 32 + 32)

            with act.Fori(0, 2) as i:
                for k in range(4):
                    gate = M[:, bass.ds(i * 4 + (HEADS + k), 1), :].rearrange("p o (h n) -> p (o h) n", n=HN)
                    act.wait_ge(tile_done, done(T_GATE + k, i, 4))
                    nc.scalar.activation(gate, acc[k % 2], ACT.Sigmoid).then_inc(acc_free, 1)
            act.drain()
            with act.Fori(0, 8) as i:
                for d in range(2):
                    act.wait_ge(tile_done, done(T_MERGE + 2 * d, i, 4))
                    act.wait_ge(merged, i * 2 + (d + 1))
                    nc.scalar.activation(sgb, acc[0], ACT.Sigmoid).then_inc(acc_free, 1)
                    act.drain().then_inc(gates_ready, 1)

            act.wait_ge(x_done, 1)
            norm_act(act, "cross", X, H)
            act.wait_ge(norm_ready, 3)
            with act.Fori(0, 4) as i:
                for k in range(4):
                    dst = M[:, bass.ds(i * 4 + k, 1), :].rearrange("p o (h n) -> p (o h) n", n=HN)
                    act.wait_ge(tile_done, done(T_MQ + k, i, 4))
                    nc.scalar.activation(dst, acc[k % 2], ACT.Copy, scale=MD ** -0.5).then_inc(acc_free, 1)
            act.drain()
            act.sem_inc(ca["oev"], 2)
            with act.Fori(0, MH) as h:
                nc.scalar.activation(qst, M[:, bass.ds(h * 4, 4), :], ACT.Copy).then_inc(ca["T"], 1)
                act.wait_ge(ca["m"], h * 2 + 1)
                for q in range(4):
                    ex = nc.scalar.activation(pm[:, q, :], psum[:, 4 + q // 2, (q % 2) * MEM:(q % 2 + 1) * MEM],
                                              ACT.Exp, bias=mst[:, q:q + 1], accum_out=mst[:, 5 + q:6 + q])
                ex.then_inc(ca["e"], 1)
                act.wait_ge(ca["m"], h * 2 + 2)
                nc.scalar.activation(pms[0:NS, :], psum[0:NS, 6, 0:MEM], ACT.Exp, bias=mst[0:NS, 4:5],
                                     accum_out=mst[0:NS, 9:10]).then_inc(ca["e"], 1)
                act.wait_ge(ca["pT"], h * 2 + 1)
                nc.scalar.activation(pmT, psum[:, 4:6, :], ACT.Copy).then_inc(ca["T"], 1)
                act.wait_ge(ca["pT"], h * 2 + 2)
                nc.scalar.activation(pmTs, psum[:, 6, 0:2 * NS].rearrange("p (b n) -> p b n", b=2),
                                     ACT.Copy).then_inc(ca["T"], 1)
                for k in range(4):
                    o = OC[:, bass.ds(h * 4 + k, 1), :].rearrange("p o n -> p (o n)")
                    act.wait_ge(ca["o"], h * 4 + (k + 1))
                    nc.scalar.activation(o[:, 0:NP_], psum[:, 2 * (k % 2), :], ACT.Copy)
                    nc.scalar.activation(o[:, NP_:NT], psum[:, 2 * (k % 2) + 1, 0:NS], ACT.Copy)\
                        .then_inc(ca["oev"], 1)
            act.wait_ge(x_done, 2)
            norm_act(act, "ffn", X, H)
            act.wait_ge(norm_ready, 4)
            with act.Fori(0, 4) as i:
                for k in range(4):
                    act.wait_ge(tile_done, done(T_PQ + k, i, 4))
                    nc.scalar.activation(halves(qps[:, k, :]), acc[k % 2], ACT.Copy).then_inc(acc_free, 1)
                    act.drain().then_inc(pk["qs"], 1)
            act.wait_ge(pk["top"], 1)
            nc.scalar.activation(best, best, ACT.Exp).then_inc(pk["gexp"], 1)
            act.wait_ge(pk["slT"], 1)
            nc.scalar.activation(slotT[:, :, 0:4 * P], psum[:, 4:7, :], ACT.Copy)
            nc.scalar.activation(slotT[:, :, 4 * P:5 * P], psum[:, 7, 0:3 * P].rearrange("p (j n) -> p j n", j=3),
                                 ACT.Copy)
            act.drain().then_inc(pk["slTe"], 1)
            act.sem_inc(pk["gev"], 4)
            for g in range(NGT):
                if g >= 2:
                    act.wait_ge(stored[g % 2], 16 * (g // 2))

                def step(n, b, col):
                    cols = slice(col, col + 4) if isinstance(col, int) else bass.ds(col, 4)
                    dst = Gs[g % 2][:, :, cols].rearrange("p a n -> p n a")
                    act.wait_ge(pk["g"], n + 1)
                    nc.scalar.activation(dst, psum[:, 4 + b, :].rearrange("p (n a) -> p n a", n=4),
                                         ACT.Copy).then_inc(pk["gev"], 1)
                gate_steps(act, g, step)
            act.wait_ge(stored[0], 16 * (NGT // 2))
            nc.scalar.activation(h_hi, H[:, :, :], ACT.Copy).then_inc(h_rounded, 1)

            def round_u(n, k, reg=None):
                act.wait_ge(u_in[k], upto(16 * (n // 2 + 1), reg, 16 * GR))
                nc.scalar.activation(u_hi[k], u_raw[k], ACT.Copy).then_inc(u_rounded, 1)

            def gelu(n, k, reg=None):
                act.wait_ge(u_done, upto(n + 1, reg, 2 * GR))
                act.wait_ge(hid_free, upto(n + 1, reg, 2 * GR))
                nc.scalar.activation(halves(hid[:, k, :]), acc[k], ACT.Gelu_apprx_tanh).then_inc(acc_free, 1)
                act.drain().then_inc(hid_ready, 1)

            def round_v(group, reg=None):
                for e in range(2):
                    act.wait_ge(v_in[e], upto(16 * (group + 1), reg, 32))
                    nc.scalar.activation(v_hi[:, :, VHALF[e]], v_raw[:, :, VHALF[e]], ACT.Copy)\
                        .then_inc(v_rounded, 1)

            round_u(0, 0)
            round_u(1, 1)
            gelu(0, 0)
            round_u(2, 0)
            gelu(1, 1)
            round_u(3, 1)
            round_v(0)
            with act.Fori(0, NG // 2 - 1) as i:
                for g in range(2):
                    gelu(GR * (g + 1), 0, i)
                    round_u(GR * (g + 2), 0, i)
                    gelu(GR * (g + 1) + 1, 1, i)
                    round_u(GR * (g + 2) + 1, 1, i)
                    round_v(g + 1, i)
            gelu(GR * (NG - 1), 0)
            gelu(GR * (NG - 1) + 1, 1)
            round_v(NG - 1)
            act.wait_ge(x_done, 3)
            norm_act(act, "final", X, H)

        @block.vector
        def _(dve):
            dve.wait_ge(consts_in, 32)
            lm = sml("lambdas").rearrange("p (a n) -> p a n", a=4)
            for a in range(2):
                nc.vector.tensor_tensor(tmp[:, 6000 + 64 * a:6064 + 64 * a], lm[:, 2 * a, :], lm[:, 2 * a + 1, :],
                                        ALU.mult)
            dve.drain()
            nc.vector.tensor_reduce(lamb[:, 0:2], tmp[:, 6000:6128].rearrange("p (a n) -> p a n", a=2), AX.X,
                                    ALU.add).then_inc(lam_parts, 1)
            nc.vector.tensor_scalar(g_diff8, sml("g_diff"), 1.0 - LAM_INIT, None, ALU.mult)
            norm_dve(dve, "mem", memT, hmT, sml("g_mem"))
            norm_dve(dve, "mix", X, H, sml("g_mix"))
            dve.wait_ge(lam_exp, 1)
            nc.vector.tensor_tensor(lamb[:, 3:4], lamb[:, 2:3], lamb[:, 3:4], ALU.subtract)
            dve.drain()
            nc.vector.tensor_scalar(nlam, lamb[:, 3:4], -1.0, -LAM_INIT, ALU.mult, ALU.add)
            dve.wait_ge(ba_parts, 1)
            gr = BG[32:40, 0:NT]
            nc.vector.tensor_tensor(gr, gr, bgt[32:40, 0:NT], ALU.add)
            dve.drain()
            nc.vector.tensor_scalar(gr, gr, lamb[32:40, 6:7], -1.0, ALU.mult, ALU.mult).then_inc(ba_done, 1)
            cw = sml("conv_w")
            for b in range(2):
                dve.wait_ge(stage_out[b], 16 * 10)
            with dve.Fori(0, HEADS) as i:
                for j in range(3):
                    n = NP_ + 3 + NS
                    dve.wait_ge(raw_ready, i * 3 + (j + 1))
                    nc.vector.tensor_scalar(yc[:, j, :], xp[:, j, 0:n], cw[:, bass.ds(i * 12 + 4 * j, 1)], None,
                                            ALU.mult)
                    for tap in range(1, 4):
                        dve.drain()
                        nc.vector.scalar_tensor_tensor(
                            out=yc[:, j, :], in0=xp[:, j, tap:tap + n],
                            scalar=cw[:, bass.ds(i * 12 + (4 * j + tap), 1)], in1=yc[:, j, :],
                            op0=ALU.mult, op1=ALU.add)
                    cs = conv_out[:, bass.ds(i, 1), 6 * j:6 * j + 6].rearrange("p o n -> p (o n)")
                    nc.vector.tensor_copy(cs[:, 0:3], xp[:, j, NP_:NP_ + 3])
                    nc.vector.tensor_copy(cs[:, 3:6], xp[:, j, NT + 3:NT + 6])
                    dve.drain().then_inc(conv_done, 1)
                dve.wait_ge(qk_root, i + 1)
                nc.vector.reciprocal(rqk[:, 0:2, 0:NT], rqk[:, 0:2, 0:NT])
                dve.drain()
                for j in range(2):
                    dst = QKV[:, bass.ds(i + j * HEADS, 1), 0:NT].rearrange("p o n -> p (o n)")
                    nc.vector.scalar_tensor_tensor(out=dst, in0=cq[:, j, :], scalar=DH ** -0.5 if j == 0 else 1.0,
                                                   in1=rqk[:, j, 0:NT], op0=ALU.mult, op1=ALU.mult)
                dve.drain().then_inc(qk_done, 1)

            beta3 = bg[:, 0:HEADS].unsqueeze(2)

            def over_heads(mask):
                return mask.unsqueeze(1).to_broadcast([CH, HEADS, CH])

            def gdn_block(c, dyn, S):
                one = c + 1
                nc.vector.tensor_copy(Kc, QKV[:, HEADS:2 * HEADS, dyn])
                nc.vector.tensor_copy(Vc, QKV[:, 2 * HEADS:3 * HEADS, dyn]).then_inc(s["c_kv"], 1)
                dve.wait_ge(s["p_bg"], one)
                nc.vector.tensor_copy(bg, b8[0][0:CH, 0:CH])
                dve.drain()
                nc.vector.tensor_tensor(gU[0:CH], bg[:, 32:40].unsqueeze(2).to_broadcast([CH, HEADS, CH]),
                                        over_heads(cst("upper", CH)), ALU.mult).then_inc(s["d_gu"], 1)
                dve.wait_ge(s["p_g"], one)
                nc.vector.tensor_copy(gcol, b8[0][0:CH, 64:72])
                dve.drain()
                nc.vector.tensor_tensor(Dd[0:CH], hc(b8[1])[0:CH],
                                        gcol.unsqueeze(2).to_broadcast([CH, HEADS, CH]), ALU.subtract)
                dve.drain()
                nc.vector.tensor_tensor(ET[0:CH], Dd[0:CH], over_heads(cst("ge", CH)), ALU.mult)
                nc.vector.tensor_tensor(ES[0:CH], Dd[0:CH], over_heads(cst("nstrict", CH)), ALU.mult)
                dve.drain().then_inc(s["d_dd"], 1)
                dve.wait_ge(s["a_exp"], one)
                dve.wait_ge(s["p_kk"], one)
                nc.vector.tensor_tensor(ES[0:CH], ES[0:CH], over_heads(cst("strict", CH)), ALU.mult)
                nc.vector.tensor_tensor(ET[0:CH], ET[0:CH], over_heads(cst("ge", CH)), ALU.mult)
                dve.drain()
                nc.vector.tensor_tensor(A[0:CH], hc(b8[2])[0:CH], ES[0:CH], ALU.mult)
                dve.drain()
                nc.vector.tensor_tensor(A[0:CH], A[0:CH], beta3.to_broadcast([CH, HEADS, CH]), ALU.mult)
                dve.drain()
                nc.vector.tensor_tensor(Bl[0:CH], A[0:CH], over_heads(levels[:, 0, :]), ALU.mult)\
                    .then_inc(s["d_a"], 1)
                nc.vector.tensor_tensor(QKT[0:CH], hc(b8[3])[0:CH], ET[0:CH], ALU.mult)
                dve.wait_ge(s["a_kvt"], c * 2 + 2)
                nc.vector.tensor_tensor(kd[0:CH], Kt[0:CH], ek.unsqueeze(2).to_broadcast([CH, HEADS, DH]), ALU.mult)
                nc.vector.tensor_tensor(kg, Kc, EG, ALU.mult)
                nc.vector.tensor_tensor(qd, Qc, EG, ALU.mult)
                idh = over_heads(ident[0:CH, 0:CH])
                dve.wait_ge(s["p_x"], c * LEVELS + 1)
                nc.vector.tensor_tensor(Rt[0:CH], idh, hc(b8[0])[0:CH], ALU.subtract)
                nc.vector.tensor_tensor(Tt[0:CH], idh, Bl[0:CH], ALU.subtract)
                dve.drain()
                nc.vector.tensor_tensor(Bl[0:CH], A[0:CH], over_heads(levels[:, 1, :]), ALU.mult)\
                    .then_inc(s["d_r"], 1)
                for lv in range(1, LEVELS):
                    dve.wait_ge(s["p_rt"], c * (LEVELS - 1) + lv)
                    nc.vector.tensor_tensor(Rt[0:CH], Rt[0:CH], hc(b8[1])[0:CH], ALU.subtract)
                    nc.vector.tensor_tensor(Tt[0:CH], Tt[0:CH], hc(b8[2])[0:CH], ALU.subtract)
                    if lv + 1 < LEVELS:
                        nc.vector.tensor_tensor(Bl[0:CH], A[0:CH], over_heads(levels[:, lv + 1, :]), ALU.mult)
                    dve.drain().then_inc(s["d_r"], 1)
                dve.wait_ge(s["p_ks"], one)
                nc.vector.tensor_tensor(Vt[0:CH], Vt[0:CH], two(4, CH), ALU.subtract)
                dve.drain()
                nc.vector.tensor_tensor(Vt[0:CH], Vt[0:CH], beta3.to_broadcast([CH, HEADS, DH]), ALU.mult)\
                    .then_inc(s["d_rr"], 1)
                dve.wait_ge(s["p_s"], one)
                nc.vector.tensor_tensor(S, S, EG[:, :, CH - 1:CH].to_broadcast([P, HEADS, DH]), ALU.mult)
                dve.drain()
                nc.vector.tensor_tensor(S, S, two(4), ALU.add)
                dve.drain().then_inc(s["d_s"], 1)
                dve.wait_ge(s["a_rto"], one)
                nc.vector.reciprocal(rto, rto)
                dve.drain()
                nc.vector.tensor_tensor(oS, oS, rto, ALU.mult)
                dve.drain()
                nc.vector.scalar_tensor_tensor(out=OA[:, :, dyn], in0=oS, scalar=sml("g_gdn"), in1=OA[:, :, dyn],
                                               op0=ALU.mult, op1=ALU.mult)
                dve.drain().then_inc(s["d_o"], 1)

            dve.wait_ge(zeroed, 3)
            with dve.Fori(0, NCH) as c:
                gdn_block(c, bass.ds(c * CH, CH), Sp)
            dve.wait_ge(state_in, 16)
            gdn_block(NCH, slice(NP_, NPAD), Ss)

            dve.wait_ge(at["dist_in"], 32)
            slopes = cst("slopes")
            with dve.Fori(0, HEADS) as h:
                slope = slopes[:, bass.ds(h, 1)]
                for q in range(QT):
                    w = P * (q + 1) if q < 4 else NT
                    rows = P if q < 4 else NS
                    for m in range(2):
                        dve.wait_ge(at["s"], h * 10 + (2 * q + m + 1))
                        if q < 4:
                            nc.vector.scalar_tensor_tensor(
                                out=sc[:, m, 0:w], in0=ndist[:, q, 0:w], scalar=slope, in1=psum[:, 4 + m, 0:w],
                                op0=ALU.mult, op1=ALU.add)
                        else:
                            nc.vector.scalar_tensor_tensor(
                                out=sc[0:NS, m, 0:NP_], in0=ndist_s[0:NS, 0:NP_], scalar=slope[0:NS],
                                in1=psum[0:NS, 4 + m, :], op0=ALU.mult, op1=ALU.add)
                            nc.vector.scalar_tensor_tensor(
                                out=sc[0:NS, m, NP_:NT], in0=ndist_s[0:NS, NP_:NT], scalar=slope[0:NS],
                                in1=psum[0:NS, 7 - m, 64 * m:64 * m + NS], op0=ALU.mult, op1=ALU.add)
                        dve.drain()
                        nc.vector.tensor_reduce(mx[0:rows, m:m + 1], sc[0:rows, m, 0:w], AX.X, ALU.max, negate=True)\
                            .then_inc(at["m"], 1)
                    dve.wait_ge(at["e"], h * 10 + (2 * q + 2))
                    nc.vector.reciprocal(rz[0:rows, :], zz[0:rows, :])
                    dve.drain()
                    nc.vector.tensor_tensor(rz[0:rows, 1:2], rz[0:rows, 1:2], nlam[0:rows], ALU.mult)
                    nc.vector.tensor_scalar(sc[0:rows, 0, 0:w], sc[0:rows, 0, 0:w], rz[0:rows, 0:1], None, ALU.mult)
                    dve.drain()
                    nc.vector.scalar_tensor_tensor(out=pr[0:rows, 0:w], in0=sc[0:rows, 1, 0:w],
                                                   scalar=rz[0:rows, 1:2], in1=sc[0:rows, 0, 0:w],
                                                   op0=ALU.mult, op1=ALU.add).then_inc(at["a"], 1)
                dst = OB[:, bass.ds(h, 1), :].rearrange("p o (h n) -> p (o h) n", n=HN)
                dve.wait_ge(at["rt"], h + 1)
                nc.vector.reciprocal(ort, ort)
                dve.drain()
                nc.vector.scalar_tensor_tensor(out=dst, in0=ob.rearrange("p (h n) -> p h n", n=HN), scalar=g_diff8,
                                               in1=ort, op0=ALU.mult, op1=ALU.mult).then_inc(at["done"], 1)

            dve.sem_inc(merged, 1)
            with dve.Fori(0, 8) as i:
                for d in range(2):
                    tile = T_MERGE + 2 * d + 1
                    dst = M[:, bass.ds(i * 2 + d, 1), :].rearrange("p o (h n) -> p (o h) n", n=HN)
                    dve.wait_ge(gates_ready, i * 2 + (d + 1))
                    dve.wait_ge(tile_done, done(tile, i, 4))
                    nc.vector.tensor_tensor(t1, dst, acc[1], ALU.mult)
                    nc.vector.tensor_tensor(sgb, sgb, aux[d % 2], ALU.mult).then_inc(acc_free, 1)
                    dve.drain()
                    nc.vector.tensor_tensor(dst, t1, sgb, ALU.add)
                    dve.drain().then_inc(merged, 1)

            def residual(first):
                with dve.Fori(0, 4) as i:
                    for k in range(4):
                        dst = X[:, bass.ds(i * 4 + k, 1), :].rearrange("p o (h n) -> p (o h) n", n=HN)
                        dve.wait_ge(tile_done, done(first + k, i, 4))
                        nc.vector.tensor_tensor(dst, dst, acc[k % 2], ALU.add).then_inc(acc_free, 1)
                dve.drain().then_inc(x_done, 1)

            dve.wait_ge(x_again, 16)
            residual(T_OUT)
            norm_dve(dve, "cross", X, H, sml("g_cross"))

            with dve.Fori(0, MH) as h:
                dve.wait_ge(ca["s"], h * 2 + 1)
                nc.vector.tensor_reduce(mst[:, 0:4], psum[:, 4:6, :].rearrange("p b (q n) -> p (b q) n", n=MEM),
                                        AX.X, ALU.max, negate=True).then_inc(ca["m"], 1)
                dve.wait_ge(ca["s"], h * 2 + 2)
                nc.vector.tensor_reduce(mst[0:NS, 4:5], psum[0:NS, 6, 0:MEM], AX.X, ALU.max, negate=True)\
                    .then_inc(ca["m"], 1)
                dve.wait_ge(ca["e"], h * 2 + 1)
                nc.vector.reciprocal(mst[:, 10:14], mst[:, 5:9])
                dve.drain()
                nc.vector.tensor_tensor(pm, pm, mst[:, 10:14].unsqueeze(2).to_broadcast([P, 4, MEM]), ALU.mult)\
                    .then_inc(ca["p"], 1)
                dve.wait_ge(ca["e"], h * 2 + 2)
                nc.vector.reciprocal(mst[0:NS, 14:15], mst[0:NS, 9:10])
                dve.drain()
                nc.vector.tensor_scalar(pms[0:NS, :], pms[0:NS, :], mst[0:NS, 14:15], None, ALU.mult)\
                    .then_inc(ca["p"], 1)
            residual(T_MO)
            norm_dve(dve, "ffn", X, H, sml("g_ffn"))

            NEG = -3.0e38
            nc.vector.memset(tv[:, 4, :], 0.0)
            nc.vector.memset(tif[:, 4, :], 0.0)
            dve.drain()
            dve.sem_inc(pk["sev"], 1)
            with dve.Fori(0, 4) as i:
                for k in range(4):
                    half, bank = k % 2, 4 + 2 * (k % 2)

                    def tiles(buf, lo, hi):
                        return [buf[0:P if q < 4 else NS, q, lo:hi] for q in range(QT)]
                    scores = [psum[:, bank, q * P:(q + 1) * P] for q in range(4)] + [last[0:NS, :]]
                    rest = tiles(work, 0, NKEY)
                    o = half * TOPK
                    first, second = tiles(tv, o, o + 8), tiles(tv, o + 8, o + 16)
                    first_i, second_i = tiles(tiu, o, o + 8), tiles(tiu, o + 8, o + 16)
                    dve.wait_ge(pk["s"], i * 4 + (k + 1))
                    nc.vector.tensor_copy(scores[4], psum[0:NS, bank + 1, 0:P])
                    dve.drain()
                    for q in range(QT):
                        nc.vector.max(first[q], scores[q])
                    dve.drain()
                    for q in range(QT):
                        nc.vector.max_index(first_i[q], first[q], scores[q])
                    for q in range(QT):
                        nc.vector.match_replace(rest[q], first[q], scores[q], NEG)
                    dve.drain().then_inc(pk["sev"], 1)
                    for q in range(QT):
                        nc.vector.max(second[q], rest[q])
                    dve.drain()
                    for q in range(QT):
                        nc.vector.max_index(second_i[q], second[q], rest[q])
                    dve.drain()
                    if half == 0:
                        continue
                    cols = bass.ds(i * (2 * TOPK) + (k // 2) * TOPK, TOPK)
                    nc.vector.tensor_copy(tif[:, 0:4, :], tiu[:, 0:4, :])
                    nc.vector.tensor_copy(tif[0:NS, 4, :], tiu[0:NS, 4, :])
                    four = [P, QT, TOPK, TOPK]
                    nc.vector.tensor_tensor(cand.rearrange("p q (a b) -> p q a b", a=TOPK),
                                            tv4[:, :, 0, :].unsqueeze(3).to_broadcast(four),
                                            tv4[:, :, 1, :].unsqueeze(2).to_broadcast(four), ALU.add)
                    dve.drain()
                    for q in range(QT):
                        nc.vector.max(bestv[:, q, 0:8], cand[:, q, :])
                    dve.drain()
                    for q in range(QT):
                        nc.vector.max_index(selu[:, 0, q, 0:8], bestv[:, q, 0:8], cand[:, q, :])
                    for q in range(QT):
                        nc.vector.match_replace(cwork[:, q, :], bestv[:, q, 0:8], cand[:, q, :], NEG)
                    dve.drain()
                    for q in range(QT):
                        nc.vector.max(bestv[:, q, 8:16], cwork[:, q, :])
                    dve.drain()
                    for q in range(QT):
                        nc.vector.max_index(selu[:, 0, q, 8:16], bestv[:, q, 8:16], cwork[:, q, :])
                    nc.vector.tensor_tensor(best[:, :, cols], bestv,
                                            bestv[:, :, 0:1].to_broadcast([P, QT, TOPK]), ALU.subtract)
                    dve.drain()
                    nc.vector.tensor_scalar(selu[:, 1], selu[:, 0], 4, None, ALU.logical_shift_right)
                    nc.vector.tensor_scalar(selu[:, 2], selu[:, 0], 15, None, ALU.bitwise_and)
                    dve.drain()
                    nc.vector.tensor_copy(abf, selu[:, 1:3])
                    eq4 = eqb.rearrange("p (q k) j -> p q k j", q=QT)
                    for a in range(2):
                        dve.drain()
                        nc.vector.tensor_tensor(eq4, abf[:, a].unsqueeze(3).to_broadcast(four),
                                                iota[:, 0:TOPK].unsqueeze(1).unsqueeze(1).to_broadcast(four),
                                                ALU.is_equal)
                        dve.drain()
                        nc.vector.tensor_tensor(eq4, eq4, tif4[:, :, a, :].unsqueeze(2).to_broadcast(four), ALU.mult)
                        dve.drain()
                        nc.vector.tensor_reduce(slots[:, a, :, cols], eq4, AX.X, ALU.add)
                    dve.drain()
            dve.sem_inc(pk["top"], 1)
            dve.wait_ge(pk["gexp"], 1)
            nc.vector.tensor_reduce(zs, best.rearrange("p q (h k) -> p (q h) k", k=TOPK), AX.X, ALU.add)
            dve.drain()
            nc.vector.reciprocal(zs, zs)
            dve.drain()
            nc.vector.tensor_tensor(slots[:, 2].rearrange("p q (h k) -> p (q h) k", k=TOPK),
                                    best.rearrange("p q (h k) -> p (q h) k", k=TOPK),
                                    zs.unsqueeze(2).to_broadcast([P, QT * HEADS, TOPK]), ALU.mult)
            dve.drain().then_inc(pk["sl"], 1)
            dve.wait_ge(pk["slTe"], 1)
            with dve.Fori(0, NT // 16) as i:
                for b in range(4):
                    key = slotT[:, 0:2, bass.ds(i * 16 + 4 * b, 4)].unsqueeze(3).to_broadcast([P, 2, 4, P])
                    row = iota.unsqueeze(1).unsqueeze(1).to_broadcast([P, 2, 4, P])
                    dve.wait_ge(pk["gev"], i * 4 + (b + 1))
                    nc.vector.tensor_tensor(OH[b], key, row, ALU.is_equal).then_inc(pk["eq"], 1)

            dve.sem_inc(hid_free, 2)
            dve.sem_inc(y_free, 2)
            dve.wait_ge(stored[1], 16 * (NGT // 2))
            dve.wait_ge(h_rounded, 1)
            nc.vector.tensor_tensor(h_lo, H[:, :, :], as_f32(h_hi), ALU.subtract)
            dve.drain().then_inc(h_split, 1)

            def split_u(n, k, reg=None, parts=(0, 1)):
                dve.wait_ge(u_rounded, upto(n + 1, reg, 2 * GR))
                for e in parts:
                    half = VHALF[e]
                    lo = nc.vector.tensor_tensor(u_lo[k][:, half], u_raw[k][:, half], as_f32(u_hi[k][:, half]),
                                                 ALU.subtract)
                if 1 in parts:
                    lo.then_inc(u_split, 1)

            def split_v(group, reg=None):
                for e in range(2):
                    dve.wait_ge(v_rounded, upto(2 * group + e + 1, reg, 4))
                    nc.vector.tensor_tensor(v_lo[:, :, VHALF[e]], v_raw[:, :, VHALF[e]],
                                            as_f32(v_hi[:, :, VHALF[e]]), ALU.subtract).then_inc(v_split, 1)

            def coefficients(group, k, reg=None):
                b = group % 2
                n = group * GR + k
                if k == 0:
                    dve.wait_ge(v_done, upto(group + 1, reg, 2))
                    dve.wait_ge(g_full[b], upto(16 * GR * (group // 2 + 1), reg, 16 * GR))
                dve.wait_ge(hid_ready, upto(n + 1, reg, 2 * GR))
                c = hid[:, k, :]
                nc.vector.tensor_tensor(c, c, gat[b][:, k, :], ALU.mult)
                dve.drain()
                nc.vector.tensor_copy(coef_hi[b][:, k, :], c)
                dve.drain()
                nc.vector.tensor_tensor(coef_lo[b][:, k, :], c, as_f32(coef_hi[b][:, k, :]), ALU.subtract)\
                    .then_inc(hid_free, 1)
                dve.drain().then_inc(coef_ready, 1)

            def expert_sum(group, chunks, reg=None):
                for d in chunks:
                    dve.wait_ge(y_full, upto(group * KD + d + 1, reg, 2 * KD))
                    dst = X[:, d, :].rearrange("p (h n) -> p h n", n=HN)
                    nc.vector.tensor_tensor(dst, dst, aux[d % 2], ALU.add).then_inc(y_free, 1)

            split_u(0, 0)
            split_u(1, 1)
            coefficients(0, 0)
            split_u(2, 0)
            coefficients(0, 1)
            split_u(3, 1)
            split_v(0)
            with dve.Fori(0, NG // 2 - 1) as i:
                for g in range(2):
                    coefficients(g + 1, 0, i)
                    expert_sum(g, range(5), i)
                    split_u(GR * (g + 2), 0, i, (0,))
                    expert_sum(g, range(5, 9), i)
                    split_u(GR * (g + 2), 0, i, (1,))
                    expert_sum(g, range(9, KD), i)
                    split_u(GR * (g + 2) + 1, 1, i)
                    coefficients(g + 1, 1, i)
                    split_v(g + 1, i)
            coefficients(NG - 1, 0)
            coefficients(NG - 1, 1)
            expert_sum(NG - 2, range(KD))
            split_v(NG - 1)
            expert_sum(NG - 1, range(KD))
            dve.drain().then_inc(x_done, 1)
            norm_dve(dve, "final", X, H, sml("g_final"))


INPUTS = [("consts", (P, N_CONST)), ("small", (P, N_SMALL)), ("xT", (P, KD, NT)), ("memT", (P, KD, MEM)),
          ("w_ba", (P, KD, 64)), ("weights", (N_STREAM, P, D)), ("uT", (NKEY, P, D)), ("v", (NKEY, P, D)),
          ("sub_keys", (P, 2 * HEADS, NKEY)), ("state_in", (P, HEADS, DH)), ("ndist", (P, 4, NP_)),
          ("ndist_s", (NS, NT)), ("cache_k", (HEADS, P, NP_)), ("cache_v", (HEADS, P, 4, DH)),
          ("cmem_k", (KD, P, MEM)), ("cmem_v", (P, 2, D))]
OUTPUTS = [("y", (P, KD, NT)), ("k_rows", (HEADS, P, NT)), ("v_rows", (HEADS, P, NT)),
           ("mem_k", (KD, P, MEM)), ("mem_v", (P, 2, D)), ("state_p", (P, HEADS, DH)),
           ("state_s", (P, HEADS, DH)), ("conv_state", (P, HEADS, 18))]


def constants():
    c = np.zeros((P, N_CONST), np.float32)

    def put(name, a):
        o, w = CONST[name]
        a = np.asarray(a, np.float32)
        c[:a.shape[0], o:o + w] = a

    i, j = np.arange(CH)[:, None], np.arange(CH)[None, :]
    put("ident", np.eye(P))
    put("ones", np.ones((P, P)))
    put("upper", i <= j)
    put("ge", i <= j)
    put("strict", i > j)
    put("nstrict", -1.0 * (i > j))
    put("levels", np.concatenate([(i // (2 << l) == j // (2 << l)) & (i // (1 << l) % 2 == 1)
                                  & (j // (1 << l) % 2 == 0) for l in range(LEVELS)], 1))
    put("iota", np.tile(np.arange(P), (P, 1)))
    put("eps", np.full((P, 2), EPS))
    put("slopes", np.tile(2.0 ** (-8.0 * (np.arange(HEADS) + 1) / HEADS), (P, 1)))
    q, k = np.arange(NP_)[:, None], np.arange(NP_)[None, :]
    dist = np.where(k // CH <= q // CH, -np.abs(q - k), -1e30).astype(np.float32)
    qs, ks = NP_ + np.arange(NS)[:, None], np.arange(NT)[None, :]
    dist_s = np.where(ks // CH <= qs // CH, -np.abs(qs - ks), -1e30).astype(np.float32)
    return c, np.ascontiguousarray(dist.reshape(4, P, NP_).transpose(1, 0, 2)), dist_s


def tiles(w):
    K, N = w.shape
    return w.reshape(K // P, P, N // P, P).transpose(2, 1, 0, 3).reshape(N // P, P, -1)


def chunked(w):
    return w.T.reshape(w.shape[1] // P, P, w.shape[0]).transpose(1, 0, 2)


def lay_out(i):
    w_in = i["w_in"][0]
    edges = np.cumsum([0, 3072, 1024, 8, 8, 1024, 1024, 1024, D, D])
    qkv, z, b, a, dq, dk, dv, ga, gb = (w_in[:, s:e] for s, e in zip(edges[:-1], edges[1:]))
    qkv_t, z_t, dq_t, dk_t, dv_t, ga_t, gb_t = map(tiles, (qkv, z, dq, dk, dv, ga, gb))
    mv = i["w_mv"][0].reshape(4, 4, P, 4, 512).transpose(3, 0, 2, 1, 4).reshape(16, P, D)
    stream = np.empty((N_STREAM, P, D), np.float32)
    stream[T_MV:T_MV + 16] = mv
    stream[T_MK:T_MK + 16] = tiles(i["w_mk"][0])
    for j in range(3):
        stream[T_GDN + j:T_DIFF:4] = qkv_t[8 * j:8 * j + 8]
    stream[T_GDN + 3:T_DIFF:4] = z_t
    for j, w in enumerate((dq_t, dk_t, dv_t, ga_t[:8])):
        stream[T_DIFF + j:T_GATE:4] = w
    stream[T_GATE:T_MERGE] = ga_t[8:]
    stream[T_MERGE:T_OUT:2] = gb_t
    stream[T_MERGE + 1:T_OUT:2, :, :D // 2] = tiles(i["w_branch_a"][0])
    stream[T_MERGE + 1:T_OUT:2, :, D // 2:] = tiles(i["w_branch_b"][0])
    for at, name in ((T_OUT, "w_out"), (T_MQ, "w_mq"), (T_MO, "w_mo"), (T_PQ, "peer_w_q")):
        stream[at:at + 16] = tiles(i[name][0])
    w_ba = np.zeros((P, KD, 64), np.float32)
    w_ba[:, :, 0:8] = b.reshape(KD, P, 8).transpose(1, 0, 2)
    w_ba[:, :, 32:40] = a.reshape(KD, P, 8).transpose(1, 0, 2)
    small = np.zeros((P, N_SMALL), np.float32)

    def put(name, v, rows=slice(0, P)):
        o, w = SMALL[name]
        small[rows, o:o + w] = v

    for name, src in (("g_mix", "norm_mix_g"), ("g_cross", "norm_cross_g"), ("g_mem", "norm_mem_g"),
                      ("g_ffn", "norm_ffn_g")):
        put(name, i[src][0].reshape(KD, P).T)
    put("g_final", i["final_norm_g"].reshape(KD, P).T)
    put("g_gdn", i["gdn_norm_g"][0][:, None])
    put("g_diff", i["diff_subln_g"][0][:, None])
    put("dt_bias", i["gdn_dt_bias"][0][:, None], slice(32, 40))
    put("a_log", i["gdn_a_log"][0][:, None], slice(32, 40))
    put("lambdas", np.concatenate([i["diff_lambda_" + n][0] for n in ("q1", "k1", "q2", "k2")])[None, :])
    put("conv_w", i["gdn_conv_w"][0].reshape(4, 3, HEADS, P).transpose(3, 2, 1, 0).reshape(P, -1))
    put("conv_state", i["state_conv"][0, 0].reshape(3, 3, HEADS, P).transpose(3, 2, 1, 0).reshape(P, -1))
    consts, ndist, ndist_s = constants()
    x = np.concatenate([i["x_prompt"][0], i["x_sample"][0]], 0)
    cv = i["cache_diff_v"][0, 0].reshape(4, P, HEADS, DH)
    return {
        "consts": consts, "small": small, "xT": chunked(x), "memT": chunked(i["mem_prompt"][0]), "w_ba": w_ba,
        "weights": stream, "uT": tiles(i["peer_u"][0].T), "v": i["peer_v"][0].reshape(NKEY, P, D),
        "sub_keys": i["peer_sub_keys"][0].reshape(2 * HEADS, NKEY, P).transpose(2, 0, 1),
        "state_in": i["state_gdn"][0, 0].transpose(1, 0, 2), "ndist": ndist, "ndist_s": ndist_s,
        "cache_k": i["cache_diff_k"][0, 0].transpose(1, 2, 0), "cache_v": cv.transpose(2, 1, 0, 3),
        "cmem_k": i["cache_mem_k"][0, 0].reshape(MEM, KD, P).transpose(1, 2, 0),
        "cmem_v": i["cache_mem_v"][0, 0].reshape(2, P, D).transpose(1, 0, 2),
    }


def kernel(**inputs):
    import concourse.bacc as bacc
    from concourse.bass_utils import run_bass_kernel_spmd

    inputs = {k: np.asarray(v) for k, v in inputs.items()}
    nc = bacc.Bacc("TRN2", target_bir_lowering=False, num_devices=1)
    laid = lay_out(inputs)
    arrays, t = {}, {}
    for name, shape in INPUTS:
        a = np.ascontiguousarray(laid[name])
        assert a.shape == tuple(shape), (name, a.shape)
        arrays["in_" + name] = a
        t[name] = nc.dram_tensor("in_" + name, a.shape, F32, kind="ExternalInput").ap()
    for name, shape in OUTPUTS:
        t[name] = nc.dram_tensor("out_" + name, shape, F32, kind="ExternalOutput").ap()
    t["gates"] = nc.dram_tensor("gates", (NT // GT, P, NKEY, GT), F32, kind="Internal").ap()
    program(nc, t)
    r = run_bass_kernel_spmd(nc, [arrays], core_ids=[0]).results[0]
    o = {name: r["out_" + name] for name, _ in OUTPUTS}

    y = o["y"].transpose(2, 1, 0).reshape(NT, D)
    k_rows = o["k_rows"].transpose(2, 0, 1)
    v_rows = o["v_rows"].transpose(2, 0, 1)
    conv = o["conv_state"].reshape(P, HEADS, 3, 2, 3).transpose(3, 4, 2, 1, 0).reshape(2, 3, 3 * HEADS * P)
    mem_k = o["mem_k"].transpose(2, 0, 1).reshape(1, 1, MEM, MH, MD)
    mem_v = o["mem_v"].transpose(1, 0, 2).reshape(1, 1, MEM, MH, MD)
    return (y[None, :NP_], y[None, NP_:], k_rows[None, None, :NP_], v_rows[None, None, :NP_],
            o["state_p"].transpose(1, 0, 2)[None, None], conv[0][None, None], mem_k, mem_v,
            k_rows[None, None, NP_:], v_rows[None, None, NP_:],
            o["state_s"].transpose(1, 0, 2)[None, None], conv[1][None, None])
```
